# Optimizing a Trainium2 kernel written in Bass

```python
import jax, jax.numpy as jnp
from jax import lax
import numpy as np

D_MODEL = 1024
BATCH = 1
SEQ = 2048
DEPTH = 1

N_MIXERS = 4
EPS = 1e-6
A_CHUNK = 128
A_WIDTH = 2048
A_GROUPS = 4
B_WIDTH = 1024
B_WINDOWS = (2, 4, 8, 16)
B_GROUPS = 4
C_WIDTH = 1024
C_HEADS = 4
C_CONV = 4
C_GATE_C = 8.0
D_WIDTH = 1024
D_CONV = 3
FFN_WIDTH = 2816
FFN_CONV = 3

kernel_name = "hybrid_interleaved_gmlp_pool_rglru_shortconv"

def rms_norm(x, g):
    xf = x.astype(jnp.float32)
    y = xf * lax.rsqrt(jnp.mean(xf * xf, axis=-1, keepdims=True) + EPS)
    return (y * g.astype(jnp.float32)).astype(x.dtype)

def causal_dwconv(x, w):
    k_taps = w.shape[0]
    s = x.shape[1]
    xp = jnp.pad(x, ((0, 0), (k_taps - 1, 0), (0, 0)))
    y = xp[:, 0:s] * w[0]
    for k in range(1, k_taps):
        y = y + xp[:, k:k + s] * w[k]
    return y

def mixer_gmlp(h, w_in, b_in, v_norm_g, w_s, b_s, w_out):
    bsz, s, _ = h.shape
    z = jax.nn.gelu(h @ w_in + b_in)
    u, v = jnp.split(z, 2, axis=-1)
    v = rms_norm(v, v_norm_g)
    gw = A_WIDTH // A_GROUPS
    v = v.reshape(bsz, s // A_CHUNK, A_CHUNK, A_GROUPS, gw)
    mask = jnp.tril(jnp.ones((A_CHUNK, A_CHUNK), dtype=bool))
    ws = jnp.where(mask, w_s, jnp.zeros_like(w_s))
    v = jnp.einsum('gts,bcsgd->bctgd', ws, v) + b_s.T[:, :, None]
    v = v.reshape(bsz, s, A_WIDTH)
    return (u * v) @ w_out

def mixer_pool(h, w_in, w_grp, b_grp, scale, w_out):
    bsz, s, _ = h.shape
    z = h @ w_in
    gw = B_WIDTH // B_GROUPS
    zf = z.astype(jnp.float32)
    csum = jnp.pad(jnp.cumsum(zf, axis=1), ((0, 0), (1, 0), (0, 0)))
    pos = jnp.arange(s)
    pooled = []
    for gi, win in enumerate(B_WINDOWS):
        c = csum[..., gi * gw:(gi + 1) * gw]
        upper = c[:, 1:]
        lower = jnp.pad(c[:, :s + 1 - win], ((0, 0), (win - 1, 0), (0, 0)))
        cnt = jnp.minimum(pos + 1, win).astype(jnp.float32)
        pooled.append((upper - lower) / cnt[None, :, None])
    p = (jnp.concatenate(pooled, axis=-1) - zf).astype(z.dtype)
    p = p.reshape(bsz, s, B_GROUPS, gw)
    y = jnp.einsum('bsgd,gde->bsge', p, w_grp) + b_grp
    y = y.reshape(bsz, s, B_WIDTH) * scale
    return y @ w_out

def mixer_rglru(h, w_in, b_in, conv_w, conv_b, w_a, b_a, w_i, b_i, lam, w_out):
    bsz, s, _ = h.shape
    z = h @ w_in + b_in
    gate, xr = jnp.split(z, 2, axis=-1)
    gate = jax.nn.gelu(gate)
    xr = causal_dwconv(xr, conv_w) + conv_b
    hw = C_WIDTH // C_HEADS
    xh = xr.reshape(bsz, s, C_HEADS, hw)
    r = jax.nn.sigmoid(jnp.einsum('bshd,hde->bshe', xh, w_a) + b_a).reshape(bsz, s, C_WIDTH)
    ig = jax.nn.sigmoid(jnp.einsum('bshd,hde->bshe', xh, w_i) + b_i).reshape(bsz, s, C_WIDTH)
    log_a = (-C_GATE_C * r.astype(jnp.float32)) * jax.nn.softplus(-lam.astype(jnp.float32))
    a = jnp.exp(log_a)
    mult = jnp.sqrt(-jnp.expm1(2.0 * log_a))
    bterm = mult * (ig * xr).astype(jnp.float32)

    def combine(left, right):
        a1, b1 = left
        a2, b2 = right
        return a1 * a2, a2 * b1 + b2

    _, hs = lax.associative_scan(combine, (a, bterm), axis=1)
    y = hs.astype(h.dtype) * gate
    return y @ w_out

def mixer_shortconv(h, w_in, conv_w, w_out):
    z = h @ w_in
    b_gate, c_gate, xv = jnp.split(z, 3, axis=-1)
    y = b_gate * causal_dwconv(c_gate * xv, conv_w)
    return y @ w_out

def conv_ffn(h, w_up, conv_w, conv_b, w_down):
    z = causal_dwconv(h @ w_up, conv_w) + conv_b
    g, v = jnp.split(z, 2, axis=-1)
    return (jax.nn.silu(g) * v) @ w_down

def setup_inputs(seed: int = 0) -> dict:
    key = jax.random.key(seed)
    keys = iter(jax.random.split(key, 64))
    n_a, n_b, n_c, n_d = (len(range(m, DEPTH, N_MIXERS)) for m in range(N_MIXERS))
    d = D_MODEL

    def nrm(shape, scale):
        return scale * jax.random.normal(next(keys), shape, jnp.float32)

    def gain(shape):
        return 1.0 + nrm(shape, 0.02)

    inp = {}
    inp["x"] = nrm((BATCH, SEQ, d), 1.0)
    inp["a_norm_g"] = gain((n_a, d))
    inp["a_w_in"] = nrm((n_a, d, 2 * A_WIDTH), d ** -0.5)
    inp["a_b_in"] = nrm((n_a, 2 * A_WIDTH), 0.02)
    inp["a_v_norm_g"] = gain((n_a, A_WIDTH))
    inp["a_w_s"] = nrm((n_a, A_GROUPS, A_CHUNK, A_CHUNK), A_CHUNK ** -0.5)
    inp["a_b_s"] = 1.0 + nrm((n_a, A_GROUPS, A_CHUNK), 0.1)
    inp["a_w_out"] = nrm((n_a, A_WIDTH, d), 0.5 * A_WIDTH ** -0.5)
    gwb = B_WIDTH // B_GROUPS
    inp["b_norm_g"] = gain((n_b, d))
    inp["b_w_in"] = nrm((n_b, d, B_WIDTH), d ** -0.5)
    inp["b_w_grp"] = nrm((n_b, B_GROUPS, gwb, gwb), gwb ** -0.5)
    inp["b_b_grp"] = nrm((n_b, B_GROUPS, gwb), 0.02)
    inp["b_scale"] = 1.0 + nrm((n_b, B_WIDTH), 0.1)
    inp["b_w_out"] = nrm((n_b, B_WIDTH, d), 0.5 * B_WIDTH ** -0.5)
    hwc = C_WIDTH // C_HEADS
    inp["c_norm_g"] = gain((n_c, d))
    inp["c_w_in"] = nrm((n_c, d, 2 * C_WIDTH), d ** -0.5)
    inp["c_b_in"] = nrm((n_c, 2 * C_WIDTH), 0.02)
    inp["c_conv_w"] = nrm((n_c, C_CONV, C_WIDTH), C_CONV ** -0.5)
    inp["c_conv_b"] = nrm((n_c, C_WIDTH), 0.02)
    inp["c_w_a"] = nrm((n_c, C_HEADS, hwc, hwc), hwc ** -0.5)
    inp["c_b_a"] = nrm((n_c, C_HEADS, hwc), 0.02)
    inp["c_w_i"] = nrm((n_c, C_HEADS, hwc, hwc), hwc ** -0.5)
    inp["c_b_i"] = nrm((n_c, C_HEADS, hwc), 0.02)
    u = jax.random.uniform(next(keys), (n_c, C_WIDTH), jnp.float32, minval=0.9, maxval=0.999)
    sgm = u ** (1.0 / C_GATE_C)
    inp["c_lambda"] = jnp.log(sgm) - jnp.log1p(-sgm)
    inp["c_w_out"] = nrm((n_c, C_WIDTH, d), C_WIDTH ** -0.5)
    inp["d_norm_g"] = gain((n_d, d))
    inp["d_w_in"] = nrm((n_d, d, 3 * D_WIDTH), d ** -0.5)
    inp["d_conv_w"] = nrm((n_d, D_CONV, D_WIDTH), D_CONV ** -0.5)
    inp["d_w_out"] = nrm((n_d, D_WIDTH, d), 0.5 * D_WIDTH ** -0.5)
    inp["ffn_norm_g"] = gain((DEPTH, d))
    inp["ffn_w_up"] = nrm((DEPTH, d, 2 * FFN_WIDTH), d ** -0.5)
    inp["ffn_conv_w"] = nrm((DEPTH, FFN_CONV, 2 * FFN_WIDTH), FFN_CONV ** -0.5)
    inp["ffn_conv_b"] = nrm((DEPTH, 2 * FFN_WIDTH), 0.02)
    inp["ffn_w_down"] = nrm((DEPTH, FFN_WIDTH, d), FFN_WIDTH ** -0.5)
    inp["final_norm_g"] = gain((d,))
    return inp

def reference(x,
              a_norm_g, a_w_in, a_b_in, a_v_norm_g, a_w_s, a_b_s, a_w_out,
              b_norm_g, b_w_in, b_w_grp, b_b_grp, b_scale, b_w_out,
              c_norm_g, c_w_in, c_b_in, c_conv_w, c_conv_b, c_w_a, c_b_a, c_w_i, c_b_i, c_lambda, c_w_out,
              d_norm_g, d_w_in, d_conv_w, d_w_out,
              ffn_norm_g, ffn_w_up, ffn_conv_w, ffn_conv_b, ffn_w_down,
              final_norm_g):
    for layer in range(DEPTH):
        m, j = layer % N_MIXERS, layer // N_MIXERS
        if m == 0:
            x = x + mixer_gmlp(rms_norm(x, a_norm_g[j]), a_w_in[j], a_b_in[j], a_v_norm_g[j],
                               a_w_s[j], a_b_s[j], a_w_out[j])
        elif m == 1:
            x = x + mixer_pool(rms_norm(x, b_norm_g[j]), b_w_in[j], b_w_grp[j], b_b_grp[j],
                               b_scale[j], b_w_out[j])
        elif m == 2:
            x = x + mixer_rglru(rms_norm(x, c_norm_g[j]), c_w_in[j], c_b_in[j], c_conv_w[j], c_conv_b[j],
                                c_w_a[j], c_b_a[j], c_w_i[j], c_b_i[j], c_lambda[j], c_w_out[j])
        else:
            x = x + mixer_shortconv(rms_norm(x, d_norm_g[j]), d_w_in[j], d_conv_w[j], d_w_out[j])
        x = x + conv_ffn(rms_norm(x, ffn_norm_g[layer]), ffn_w_up[layer], ffn_conv_w[layer],
                         ffn_conv_b[layer], ffn_w_down[layer])
    return rms_norm(x, final_norm_g)


_drawn_inputs = setup_inputs


def setup_inputs(seed=0):
    import zlib

    import numpy as np

    out = dict(_drawn_inputs(seed))
    spreads = {}
    factors = {'a_norm_g': 5.336,
     'a_b_in': 5.859,
     'a_v_norm_g': 8.0,
     'ffn_norm_g': 4.129,
     'ffn_conv_b': 4.114,
     'final_norm_g': 2.852}
    for name, (base, spread) in spreads.items():
        noise = np.random.default_rng([zlib.crc32(name.encode()), seed]).standard_normal(out[name].shape)
        drawn = base * np.exp(spread * noise) if base else spread * noise
        out[name] = __import__('jax').numpy.asarray(drawn.astype(out[name].dtype))
    for name, factor in factors.items():
        out[name] = (out[name] * factor).astype(out[name].dtype)
    return out
```

```python
import concourse.bass as bass
from concourse import mybir
from contextlib import ExitStack

P = 128
NORM_EPS = 1e-6


def gmlp_ffn_trunk(nc, x, a_norm_g, a_w_in, a_b_in, a_v_norm_g, a_w_s, a_b_s, a_w_out,
                   ffn_norm_g, ffn_w_up, ffn_conv_w, ffn_conv_b, ffn_w_down, final_norm_g, out):
    f32 = mybir.dt.float32
    f32r = mybir.dt.float32r
    ACT = mybir.ActivationFunctionType
    ALU = mybir.AluOpType
    ds = bass.ds

    SEQ, D = x.shape[1], x.shape[2]
    AW = a_w_out.shape[1]
    FW = ffn_w_down.shape[1]
    GROUPS = a_w_s.shape[1]
    COLS = 512
    CH = COLS // P
    BLOCKS = SEQ // COLS
    KT = D // P
    FT = FW // P
    UNITS = FT // 2
    HALF_UNITS = (6, 5)
    assert AW == GROUPS * COLS and KT == 8 and UNITS == sum(HALF_UNITS) and SEQ % COLS == 0

    Q = KT // 2
    V_PAIR = 0
    HALF_PAIR = 4 * Q
    HALF_PAIRS = 4 * Q
    UP_PAIR = (HALF_PAIR + 2 * HALF_PAIRS,)
    DOWN_PAIR = (UP_PAIR[0] + Q * HALF_UNITS[0],)
    UP_PAIR += (DOWN_PAIR[0] + 2 * HALF_UNITS[0],)
    DOWN_PAIR += (UP_PAIR[1] + Q * HALF_UNITS[1],)
    PAIRS = DOWN_PAIR[1] + 2 * HALF_UNITS[1]
    RAW = 4
    SPLIT = 2
    assert PAIRS % SPLIT == 0
    FILLS = [len(range(s, PAIRS, RAW)) for s in range(RAW)]

    END = {f"v{f}": V_PAIR + Q * (f + 1) for f in range(GROUPS)}
    for f in range(GROUPS):
        END[f"u{f}"] = HALF_PAIR + HALF_PAIRS * (f // 2) + Q * (f % 2 + 1)
    for half in range(2):
        for dh in range(2):
            END[f"o{half}{dh}"] = HALF_PAIR + HALF_PAIRS * half + Q * (3 + dh)
            END[f"d{half}{dh}"] = DOWN_PAIR[half] + HALF_UNITS[half] * (dh + 1)
    DV, n = {}, 0
    for name, banks in (("v0", 4), ("v1", 4), ("v2", 4), ("v3", 4), ("m0", 4), ("m1", 4), ("o00", 4),
                        ("o01", 4), ("m2", 4), ("m3", 4), ("o10", 4), ("o11", 4), ("T2", 8),
                        ("d00", 4), ("d01", 4), ("T1a", 4), ("d10", 4), ("d11", 4), ("T1b", 4)):
        DV[name] = n
        n += banks
    DV_BLOCK = n
    AC_UP = 4 * GROUPS
    AC_BLOCK = AC_UP + 4 * UNITS
    T_FIRST = KT
    T_BLOCK = 2 * KT

    ctx = ExitStack()
    with ctx:
        def sb(name, shape, dt=f32):
            return ctx.enter_context(nc.sbuf_tensor(name, shape, dt))

        def sem(name):
            return ctx.enter_context(nc.semaphore(name))

        w_raw = sb("w_raw", [P, RAW, 2, COLS])
        w_hi = sb("w_hi", [P, SPLIT, 2, COLS], f32r)
        w_lo = sb("w_lo", [P, SPLIT, 2, COLS], f32r)
        h_hi = sb("h_hi", [P, KT, COLS], f32r)
        h_lo = sb("h_lo", [P, KT, COLS], f32r)
        TILES = 2 * max(HALF_UNITS)
        a_hi = sb("a_hi", [P, TILES, COLS], f32r)
        a_lo = sb("a_lo", [P, TILES, COLS], f32r)
        VS = TILES - CH
        region = sb("region", [P, CH * AW + 8])
        v = region[:, 0:CH * AW].rearrange("p (c f) -> p c f", c=CH)
        rows = region[:, 0:CH * D].rearrange("p (c d) -> p c d", c=CH)
        conv = region[:, CH * D:CH * D + 4 * COLS].rearrange("p (t n) -> p t n", t=4)
        z = region[:, CH * D + 4 * COLS:CH * AW + 8].rearrange("p (t n) -> p t n", t=4)
        res = sb("res", [P, CH, D])
        u_gelu = sb("u_gelu", [P, 4, COLS])
        mixed = sb("mixed", [P, COLS])
        squares = sb("squares", [P, D])
        ws_t = sb("ws_t", [P, GROUPS, P])
        ws_hi = sb("ws_hi", [P, CH, P], f32r)
        ws_lo = sb("ws_lo", [P, CH, P], f32r)
        history = sb("history", [P, UNITS, 4, 2])
        ident = sb("ident", [P, P])
        by_feature = sb("by_feature", [P, 2 * KT + 2 * (AW // P)])
        g_mix = by_feature[:, 0:KT]
        g_ffn = by_feature[:, KT:2 * KT]
        b_u = by_feature[:, 2 * KT:2 * KT + AW // P]
        g_v = by_feature[:, 2 * KT + AW // P:2 * KT + 2 * (AW // P)]
        conv_par = sb("conv_par", [P, 4, 2, FT])
        conv_w = conv_par[:, 0:3]
        conv_b = conv_par[:, 3]
        b_v = sb("b_v", [P, AW])
        b_s = sb("b_s", [P, GROUPS * P])
        g_out = sb("g_out", [P, D])
        ss_v = sb("ss_v", [P, GROUPS, CH])
        ss_res = sb("ss_res", [P, 2, CH])
        ss_x = sb("ss_x", [P, CH])
        ss_out = sb("ss_out", [P, CH])
        ss_pair = sb("ss_pair", [P, 2, CH])
        ss_sum = sb("ss_sum", [P, CH])
        mean = sb("mean", [P, CH])
        minus_half = sb("minus_half", [P, CH])
        r_v = sb("r_v", [P, CH])
        r_res = sb("r_res", [P, CH])
        r_x = sb("r_x", [P, CH])
        r_out = sb("r_out", [P, CH])

        staged_ws = u_gelu[:, 0, :]
        staged_par = u_gelu[:, 1, 0:3 * P].rearrange("p (i n) -> p i n", i=3)
        CONV_ROWS = 2 * 2 * FT

        ps = ctx.enter_context(nc.psum_tensor("ps", [P, 8, COLS], f32))

        w_loaded = [sem(f"w_loaded{s}") for s in range(RAW)]
        w_hi_ready = sem("w_hi_ready")
        w_ready = sem("w_ready")
        w_used = sem("w_used")
        mix_done = sem("mix_done")
        transposed = sem("transposed")
        dve_drained = sem("dve_drained")
        act_drained = sem("act_drained")
        h_hi_ready = sem("h_hi_ready")
        v_gelu = sem("v_gelu")
        vs_hi_ready = sem("vs_hi_ready")
        vs_ready = sem("vs_ready")
        ws_hi_ready = sem("ws_hi_ready")
        ws_ready = sem("ws_ready")
        uv_done = sem("uv_done")
        uv_hi_ready = sem("uv_hi_ready")
        uv_ready = sem("uv_ready")
        history_in = sem("history_in")
        z_ready = sem("z_ready")
        history_out = sem("history_out")
        tapped = sem("tapped")
        silu_done = sem("silu_done")
        gv_done = sem("gv_done")
        gv_hi_ready = sem("gv_hi_ready")
        gv_ready = sem("gv_ready")
        squared = sem("squared")
        r_v_ready = sem("r_v_ready")
        r_res_ready = sem("r_res_ready")
        r_x_ready = sem("r_x_ready")
        r_out_ready = sem("r_out_ready")
        x_scaled = sem("x_scaled")
        res_scaled_dve = sem("res_scaled_dve")
        res_scaled_act = sem("res_scaled_act")
        pool_step = sem("pool_step")
        pool_waits = sem("pool_waits")
        y_done = sem("y_done")
        x_loaded = sem("x_loaded")
        res_loaded = sem("res_loaded")
        y_stored = sem("y_stored")
        consts = sem("consts")
        par_loaded = sem("par_loaded")
        turned = sem("turned")
        set_up = sem("set_up")
        ws_loaded = sem("ws_loaded")
        made = sem("made")

        block = ctx.enter_context(nc.Block())

        SQ_V, SQ_RES, SQ_X, SQ_OUT = 0, 4 * GROUPS, 4 * GROUPS + 2 * CH, 4 * GROUPS + 3 * CH
        SQ_BLOCK = SQ_OUT + CH
        SQ_FIRST = CH
        START = 1
        CONSTS = 3
        PARS = 8

        STEP_V, STEP_RES, STEP_X, STEP_OUT, STEP_Y = 0, 3, 5, 6, 7
        STEP_BLOCK = STEP_Y + CH
        STEP_FIRST = 1

        @block.sync
        def _(sp):
            def load(b, j, src, opens_block=False):
                slot = j[1] % RAW
                at = b * PAIRS + j[0] + j[1]
                if opens_block:
                    sp.wait_ge(w_ready, at + RAW - 1)
                else:
                    sp.wait_ge(w_ready, at + 1)
                for t in range(2):
                    sp.dma_start(w_raw[:, slot, t, :] if len(src[t].shape) == 2 else
                                 w_raw[:, slot, t, :].rearrange("p (h n) -> p h n", h=2),
                                 src[t]).then_inc(w_loaded[slot], 16)

            w_in, w_out = a_w_in[0], a_w_out[0]
            w_up = ffn_w_up[0].rearrange("k (h n) -> k h n", h=2)
            w_down = ffn_w_down[0]

            def in_tiles(q, col):
                return [w_in[(2 * q + t) * P:(2 * q + t + 1) * P, ds(col, COLS)] for t in range(2)]

            with sp.Fori(0, BLOCKS) as b:
                for f in range(GROUPS):
                    for q in range(Q):
                        load(b, (0, V_PAIR + Q * f + q), in_tiles(q, AW + f * COLS),
                             f == 0 and q < PAIRS % RAW)
                with sp.Fori(0, 2) as half:
                    first = half * HALF_PAIRS
                    for g in range(2):
                        for q in range(Q):
                            load(b, (first, HALF_PAIR + Q * g + q), in_tiles(q, half * (2 * COLS) + g * COLS))
                    for dh in range(2):
                        for q in range(Q):
                            row = half * (KT * P)
                            load(b, (first, HALF_PAIR + Q * (2 + dh) + q),
                                 [w_out[ds(row + (2 * q + t) * P, P), dh * COLS:(dh + 1) * COLS] for t in range(2)])
                for half in range(2):
                    base = sum(HALF_UNITS[:half])
                    with sp.Fori(0, HALF_UNITS[half]) as i:
                        for q in range(Q):
                            load(b, (i * Q, UP_PAIR[half] + q),
                                 [w_up[(2 * q + t) * P:(2 * q + t + 1) * P, :, ds(i * (2 * P) + base * 2 * P, 2 * P)]
                                  for t in range(2)])
                    for dh in range(2):
                        for i in range(HALF_UNITS[half]):
                            row = (base + i) * 2 * P
                            load(b, (0, DOWN_PAIR[half] + dh * HALF_UNITS[half] + i),
                                 [w_down[row + t * P:row + (t + 1) * P, dh * COLS:(dh + 1) * COLS] for t in range(2)])
            for q in range(SPLIT):
                load(BLOCKS, (0, q), in_tiles(q, AW), True)

        @block.scalar
        def _(act):
            def split(b, mult, off):
                slot, half_slot = off % RAW, off % SPLIT
                if off >= PAIRS and isinstance(mult, int):
                    slot = off - PAIRS
                    fills = b * FILLS[slot] + FILLS[slot] + 1
                else:
                    fills = b * FILLS[slot] + mult // RAW + off // RAW + 1 if isinstance(mult, int) else \
                        b * FILLS[slot] + mult + off // RAW + 1
                    mult = mult if isinstance(mult, int) else mult * RAW
                act.wait_ge(w_loaded[slot], fills * 32)
                act.wait_ge(w_used, b * PAIRS + mult + off + 1)
                nc.scalar.activation(w_hi[:, half_slot], w_raw[:, slot], ACT.Copy).then_inc(w_hi_ready, 1)

            def square(b, nth, dst, src):
                if b is not None:
                    act.wait_ge(squared, b * SQ_BLOCK + SQ_FIRST + nth)
                elif nth:
                    act.wait_ge(squared, nth)
                nc.scalar.activation(squares[:, 0:src.shape[-1]], src, ACT.Square, accum_out=dst).then_inc(squared, 1)

            def on_every_partition(dst, src, done):
                act.dma_start(dst, src.partition_broadcast(P)).then_inc(done, 16)

            def h_tile(bank, k, gain, nth):
                act.wait_ge(transposed, nth)
                nc.scalar.activation(h_hi[:, k, :], ps[:, bank, :], ACT.Copy,
                                     scale=gain[:, k:k + 1]).then_inc(h_hi_ready, 1)

            def v_drain(b, f, c):
                act.wait_ge(dve_drained, b * DV_BLOCK + T_FIRST + DV[f"v{f}"] + c + 1)
                tile = v[:, c, f * COLS:(f + 1) * COLS]
                nc.scalar.activation(tile, tile, ACT.Gelu_apprx_tanh).then_inc(v_gelu, 1)
                act.wait_ge(v_gelu, b * (4 * GROUPS) + 4 * f + c + 1)
                square(b, SQ_V + 4 * f + c, ss_v[:, f, c:c + 1], tile)

            def uv_hi(b, f, t):
                nth = 4 * f + t
                act.wait_ge(uv_done, b * (4 * GROUPS) + nth + 1)
                nc.scalar.activation(a_hi[:, 4 * (f % 2) + t, :], mixed[:, :], ACT.Copy).then_inc(uv_hi_ready, 1)

            def ffn_z(b, i, par, end):
                act.wait_ge(w_used, b * PAIRS + SPLIT + end)
                act.wait_ge(history_in, b * UNITS + i + 1)
                nc.scalar.activation(z[:, :, 2:COLS + 2], ps[:, 4 * par:4 * par + 4, :], ACT.Copy).then_inc(z_ready, 1)
                act.wait_ge(gv_ready, b * UNITS + START + i)
                for t in range(2):
                    tap_last(i, par, t)

            def tap_last(i, par, t):
                tile = 2 * i + t % 2
                nc.scalar.activation(conv[:, t, :], ps[:, 4 * par + t, :], ACT.Identity,
                                     scale=conv_w[:, 2, t // 2, ds(tile, 1)],
                                     bias=conv_b[:, t // 2, ds(tile, 1)]).then_inc(act_drained, 1)

            def ffn_silu(b, i):
                act.wait_ge(tapped, b * (8 * UNITS) + START + i * 8 + 4)
                nc.scalar.activation(conv[:, 0:2, :], conv[:, 0:2, :], ACT.Silu).then_inc(silu_done, 1)

            def ffn_hi(b, i, tile):
                act.wait_ge(gv_done, b * UNITS + i + 1)
                nc.scalar.activation(a_hi[:, ds(tile, 2), :], conv[:, 0:2, :], ACT.Copy).then_inc(gv_hi_ready, 1)

            def ffn_piece(b, i, half, par, tile, q):
                if q == 0:
                    ffn_z(b, i, par, UP_PAIR[half] + Q * (i - sum(HALF_UNITS[:half]) + 1))
                elif q == 1:
                    for t in (2, 3):
                        tap_last(i, par, t)
                elif q == 2:
                    ffn_silu(b, i)
                elif q == 3:
                    ffn_hi(b, i, tile)

            act.dma_start(u_gelu[:, 0, :].rearrange("p (g s) -> p g s", g=GROUPS),
                          a_w_s[0].rearrange("g t s -> t g s")).then_inc(ws_loaded, 16)
            row = 0
            for src in (a_norm_g[0], ffn_norm_g[0], a_b_in[0, 0:AW], a_v_norm_g[0]):
                tiles = src.rearrange("(k p) -> k p", p=P)
                act.dma_start(staged_par[row:row + tiles.shape[0], 0, :], tiles).then_inc(par_loaded, 16)
                row += tiles.shape[0]
            for i, src in enumerate((ffn_conv_w[0, 0], ffn_conv_w[0, 1], ffn_conv_w[0, 2], ffn_conv_b[0])):
                row = i % 2 * 2 * FT
                act.dma_start(staged_par[row:row + 2 * FT, 1 + i // 2, :],
                              src.rearrange("(k p) -> k p", p=P)).then_inc(par_loaded, 16)
            on_every_partition(b_v[:, :], a_b_in[0, AW:2 * AW], consts)
            on_every_partition(b_s[:, :], a_b_s[0].rearrange("g t -> (g t)"), consts)
            on_every_partition(g_out[:, :], final_norm_g, consts)
            for c in range(CH):
                act.wait_ge(x_loaded, 16 * CH)
                square(None, c, ss_x[:, c:c + 1], rows[:, c, :])
            split(0, 0, 0)
            split(0, 0, 1)
            act.wait_ge(set_up, 4)
            for k in range(KT):
                h_tile(k, k, g_mix, k + 1)

            with act.Fori(0, BLOCKS) as b:
                def drained(name, nth):
                    return b * DV_BLOCK + T_FIRST + DV[name] + nth

                for f in range(GROUPS):
                    for q in range(Q):
                        if f or q:
                            split(b, 0, V_PAIR + Q * f + q + 1)
                        if f:
                            v_drain(b, f - 1, q)
                for f in range(GROUPS):
                    half = f // 2
                    for q in range(Q):
                        split(b, 0, HALF_PAIR + HALF_PAIRS * half + Q * (f % 2) + q + 1)
                        if f == 0:
                            v_drain(b, GROUPS - 1, q)
                        elif f % 2:
                            uv_hi(b, f - 1, q)
                        if f:
                            act.wait_ge(mix_done, b * GROUPS + f)
                        act.wait_ge(v_gelu, b * (4 * GROUPS) + 4 * f + q + 1)
                        nc.scalar.activation(a_hi[:, VS + q, :], v[:, q, f * COLS:(f + 1) * COLS],
                                             ACT.Copy).then_inc(vs_hi_ready, 1)
                    act.wait_ge(r_v_ready, b + 1)
                    for c in range(CH):
                        nc.scalar.activation(ws_hi[:, c, :], ws_t[:, f, :], ACT.Copy,
                                             scale=r_v[:, c:c + 1]).then_inc(ws_hi_ready, 1)
                    act.wait_ge(w_used, b * PAIRS + SPLIT + END[f"u{f}"])
                    if f:
                        act.wait_ge(uv_done, b * (4 * GROUPS) + 4 * f)
                    for t in range(4):
                        nc.scalar.activation(u_gelu[:, t, :], ps[:, t, :], ACT.Gelu_apprx_tanh,
                                             bias=b_u[:, 4 * f + t:4 * f + t + 1]).then_inc(act_drained, 1)
                    if f % 2:
                        for dh in range(2):
                            for q in range(Q):
                                split(b, 0, HALF_PAIR + HALF_PAIRS * half + Q * (2 + dh) + q + 1)
                                if dh == 0 and q < 2:
                                    uv_hi(b, f, 2 * q)
                                    uv_hi(b, f, 2 * q + 1)
                                if dh == 1 and half == 1:
                                    act.wait_ge(dve_drained, drained("o10", q + 1))
                                    square(b, SQ_RES + q, ss_res[:, 0, q:q + 1], res[:, q, 0:COLS])

                for c in range(CH):
                    act.wait_ge(dve_drained, drained("o11", c + 1))
                    square(b, SQ_RES + CH + c, ss_res[:, 1, c:c + 1], res[:, c, COLS:D])
                act.wait_ge(r_res_ready, b + 1)
                for c in range(2, CH):
                    nc.scalar.activation(rows[:, c, :], res[:, c, :], ACT.Copy,
                                         scale=r_res[:, c:c + 1]).then_inc(res_scaled_act, 1)
                for k in range(KT):
                    h_tile(k, k, g_ffn, b * T_BLOCK + T_FIRST + k + 1)
                    if k == 3:
                        split(b, 0, UP_PAIR[0] + 1)

                for half in range(2):
                    base = sum(HALF_UNITS[:half])
                    for q in range(Q):
                        if half or q:
                            split(b, 0, UP_PAIR[half] + q + 1)
                    n_loops = (HALF_UNITS[half] - 1) // 2
                    with act.Fori(0, n_loops) as i2:
                        for par in range(2):
                            for q in range(Q):
                                split(b, i2 * 2, UP_PAIR[half] + Q * (par + 1) + q + 1)
                                ffn_piece(b, i2 * 2 + base + par, half, par, i2 * 4 + 2 * par, q)
                    if HALF_UNITS[half] % 2 == 0:
                        i = HALF_UNITS[half] - 2
                        for q in range(Q):
                            split(b, 0, UP_PAIR[half] + Q * (i + 1) + q + 1)
                            ffn_piece(b, base + i, half, i % 2, 2 * i, q)
                    i = HALF_UNITS[half] - 1
                    for dh in range(2):
                        for q in range(HALF_UNITS[half]):
                            split(b, 0, DOWN_PAIR[half] + dh * HALF_UNITS[half] + q + 1)
                            if half and dh == 0 and q == 3:
                                for k in range(4):
                                    h_tile(k, k, g_mix, b * T_BLOCK + T_FIRST + KT + k + 1)
                            if dh == 0 and q < 4:
                                ffn_piece(b, base + i, half, i % 2, 2 * i, q)
                            if half == 0 and dh == 1 and q < CH:
                                if q == 0:
                                    act.wait_ge(x_loaded, (b + 2) * (16 * CH))
                                square(b, SQ_X + q, ss_x[:, q:q + 1], rows[:, q, :])
                for k in range(4, KT):
                    h_tile(k, k, g_mix, b * T_BLOCK + T_FIRST + KT + k + 1)
                split(b, 0, PAIRS + 1)
                for c in range(CH):
                    act.wait_ge(dve_drained, drained("d11", c + 1))
                    square(b, SQ_OUT + c, ss_out[:, c:c + 1], res[:, c, :])

        @block.vector
        def _(dve):
            def split(b, mult, off):
                dve.wait_ge(w_hi_ready, b * PAIRS + mult + off + 1)
                nc.vector.tensor_tensor(w_lo[:, off % SPLIT], w_raw[:, off % RAW if off < PAIRS else off - PAIRS],
                                        w_hi[:, off % SPLIT].bitcast(f32), ALU.subtract).then_inc(w_ready, 1)

            def h_tile(bank, k, gain, nth):
                dve.wait_ge(h_hi_ready, nth)
                nc.vector.scalar_tensor_tensor(out=h_lo[:, k, :], in0=ps[:, bank, :], scalar=gain[:, k:k + 1],
                                               in1=h_hi[:, k, :].bitcast(f32), op0=ALU.mult,
                                               op1=ALU.subtract).then_inc(dve_drained, 1)

            def v_bias(b, f, c):
                dve.wait_ge(w_used, b * PAIRS + SPLIT + END[f"v{f}"])
                if f == 0:
                    dve.wait_ge(history_out, b * UNITS + START)
                nc.vector.tensor_tensor(v[:, c, f * COLS:(f + 1) * COLS], ps[:, 4 * (f % 2) + c, :],
                                        b_v[:, f * COLS:(f + 1) * COLS], ALU.add).then_inc(dve_drained, 1)

            def uv(b, f, t):
                nth = b * (4 * GROUPS) + 4 * f + t
                dve.wait_ge(mix_done, b * GROUPS + f + 1)
                dve.wait_ge(uv_ready, nth + START)
                nc.vector.scalar_tensor_tensor(
                    out=mixed[:, :].rearrange("p (c t) -> p c t", c=CH),
                    in0=ps[:, 4 + t, :].rearrange("p (c t) -> p c t", c=CH),
                    scalar=g_v[:, 4 * f + t:4 * f + t + 1],
                    in1=b_s[:, f * P:(f + 1) * P].unsqueeze(1).to_broadcast([P, CH, P]),
                    op0=ALU.mult, op1=ALU.add).then_inc(dve_drained, 1)
                dve.wait_ge(dve_drained, b * DV_BLOCK + T_FIRST + DV[f"m{f}"] + t + 1)
                dve.wait_ge(act_drained, b * AC_BLOCK + 4 * f + t + 1)
                nc.vector.tensor_tensor(mixed[:, :], mixed[:, :], u_gelu[:, t, :], ALU.mult).then_inc(uv_done, 1)
                dve.wait_ge(uv_hi_ready, nth + 1)
                nc.vector.tensor_tensor(a_lo[:, 4 * (f % 2) + t, :], mixed[:, :],
                                        a_hi[:, 4 * (f % 2) + t, :].bitcast(f32), ALU.subtract).then_inc(uv_ready, 1)

            def add_res(b, name, par, dh, c):
                dve.wait_ge(w_used, b * PAIRS + SPLIT + END[name])
                cols = res[:, c, dh * COLS:(dh + 1) * COLS]
                nc.vector.tensor_tensor(cols, cols, ps[:, 4 * par + c, :], ALU.add).then_inc(dve_drained, 1)

            def taps(b, i, pair):
                at = b * (8 * UNITS) + START + i * 8 + 4 * pair
                dve.wait_ge(z_ready, b * UNITS + i + 1)
                dve.wait_ge(act_drained, b * AC_BLOCK + AC_UP + i * 4 + 2 * pair + 2)
                for tap in (1, 0):
                    for t in (2 * pair, 2 * pair + 1):
                        if tap == 0:
                            dve.wait_ge(tapped, at + t % 2 + 1)
                        nc.vector.scalar_tensor_tensor(
                            out=conv[:, t, :], in0=z[:, t, tap:tap + COLS],
                            scalar=conv_w[:, tap, t // 2, ds(2 * i + t % 2, 1)], in1=conv[:, t, :],
                            op0=ALU.mult, op1=ALU.add).then_inc(tapped, 1)

            def ffn_piece(b, i, tile, q):
                if q == 1:
                    taps(b, i, 0)
                elif q == 2:
                    taps(b, i, 1)
                elif q == 3:
                    dve.wait_ge(silu_done, b * UNITS + i + 1)
                    dve.wait_ge(tapped, b * (8 * UNITS) + START + i * 8 + 8)
                    nc.vector.tensor_tensor(conv[:, 0:2, :], conv[:, 0:2, :], conv[:, 2:4, :],
                                            ALU.mult).then_inc(gv_done, 1)
                    dve.wait_ge(gv_hi_ready, b * UNITS + i + 1)
                    nc.vector.tensor_tensor(a_lo[:, ds(tile, 2), :], conv[:, 0:2, :],
                                            a_hi[:, ds(tile, 2), :].bitcast(f32), ALU.subtract).then_inc(gv_ready, 1)

            nc.vector.memset(minus_half[:, :], -0.5).then_inc(made, 1)
            nc.vector.memset(history[:, :, :, :], 0.0).then_inc(made, 1)
            dve.sem_inc(w_ready, RAW)
            dve.sem_inc(tapped, START)
            dve.sem_inc(gv_ready, START)
            dve.sem_inc(uv_ready, START)
            dve.wait_ge(turned, 1)
            nc.vector.tensor_copy(by_feature[:, :], ps[:, 1, 0:by_feature.shape[1]]).then_inc(set_up, 1)
            for i in range(2):
                nc.vector.tensor_copy(conv_par[:, 2 * i:2 * i + 2].rearrange("p a h j -> p (a h j)"),
                                      ps[:, 1, (i + 1) * P:(i + 1) * P + CONV_ROWS]).then_inc(set_up, 1)
            dve.wait_ge(turned, 2)
            nc.vector.tensor_copy(ws_t[:, :, :], ps[:, 0, :].rearrange("p (g s) -> p g s", g=GROUPS)).then_inc(set_up, 1)
            dve.wait_ge(set_up, 4)
            split(0, 0, 0)
            split(0, 0, 1)
            dve.wait_ge(consts, 16 * CONSTS)
            for k in range(KT):
                h_tile(k, k, g_mix, k + 1)
            with dve.Fori(0, BLOCKS) as b:
                for f in range(GROUPS):
                    for q in range(Q):
                        if f or q:
                            split(b, 0, V_PAIR + Q * f + q + 1)
                        if f:
                            v_bias(b, f - 1, q)
                for f in range(GROUPS):
                    half = f // 2
                    for q in range(Q):
                        split(b, 0, HALF_PAIR + HALF_PAIRS * half + Q * (f % 2) + q + 1)
                        if f == 0:
                            v_bias(b, GROUPS - 1, q)
                        elif f % 2:
                            uv(b, f - 1, q)
                        else:
                            add_res(b, "o01", 1, 1, q)
                        dve.wait_ge(vs_hi_ready, b * (4 * GROUPS) + 4 * f + q + 1)
                        nc.vector.tensor_tensor(a_lo[:, VS + q, :], v[:, q, f * COLS:(f + 1) * COLS],
                                                a_hi[:, VS + q, :].bitcast(f32), ALU.subtract).then_inc(vs_ready, 1)
                    for c in range(CH):
                        dve.wait_ge(ws_hi_ready, b * (4 * GROUPS) + 4 * f + c + 1)
                        nc.vector.scalar_tensor_tensor(out=ws_lo[:, c, :], in0=ws_t[:, f, :], scalar=r_v[:, c:c + 1],
                                                       in1=ws_hi[:, c, :].bitcast(f32), op0=ALU.mult,
                                                       op1=ALU.subtract).then_inc(ws_ready, 1)
                    if f % 2:
                        for dh in range(2):
                            for q in range(Q):
                                split(b, 0, HALF_PAIR + HALF_PAIRS * half + Q * (2 + dh) + q + 1)
                                if dh == 0 and q < 2:
                                    uv(b, f, 2 * q)
                                    uv(b, f, 2 * q + 1)
                                if dh == 1:
                                    if half == 0 and q == 0:
                                        dve.wait_ge(res_loaded, (b + 1) * (16 * CH))
                                    add_res(b, f"o{half}0", 0, 0, q)
                for c in range(CH):
                    add_res(b, "o11", 1, 1, c)
                dve.wait_ge(r_res_ready, b + 1)
                for c in range(2):
                    nc.vector.tensor_scalar(rows[:, c, :], res[:, c, :], r_res[:, c:c + 1], None,
                                            ALU.mult).then_inc(res_scaled_dve, 1)
                for k in range(KT):
                    h_tile(k, k, g_ffn, b * T_BLOCK + T_FIRST + k + 1)
                    if k == 3:
                        split(b, 0, UP_PAIR[0] + 1)
                for half in range(2):
                    base = sum(HALF_UNITS[:half])
                    for q in range(Q):
                        if half or q:
                            split(b, 0, UP_PAIR[half] + q + 1)
                        if half:
                            add_res(b, "d01", 1, 1, q)
                    n_loops = (HALF_UNITS[half] - 1) // 2
                    with dve.Fori(0, n_loops) as i2:
                        for par in range(2):
                            for q in range(Q):
                                split(b, i2 * (2 * Q), UP_PAIR[half] + Q * (par + 1) + q + 1)
                                ffn_piece(b, i2 * 2 + base + par, i2 * 4 + 2 * par, q)
                    if HALF_UNITS[half] % 2 == 0:
                        i = HALF_UNITS[half] - 2
                        for q in range(Q):
                            split(b, 0, UP_PAIR[half] + Q * (i + 1) + q + 1)
                            ffn_piece(b, base + i, 2 * i, q)
                    i = HALF_UNITS[half] - 1
                    for dh in range(2):
                        for q in range(HALF_UNITS[half]):
                            split(b, 0, DOWN_PAIR[half] + dh * HALF_UNITS[half] + q + 1)
                            if half and dh == 0 and q == 3:
                                for k in range(4):
                                    h_tile(k, k, g_mix, b * T_BLOCK + T_FIRST + KT + k + 1)
                            if dh == 0 and q < 4:
                                ffn_piece(b, base + i, 2 * i, q)
                            if dh == 1 and q < CH:
                                add_res(b, f"d{half}0", half, 0, q)
                for c in range(CH):
                    add_res(b, "d11", 0, 1, c)
                for k in range(4, KT):
                    h_tile(k, k, g_mix, b * T_BLOCK + T_FIRST + KT + k + 1)
                split(b, 0, PAIRS + 1)

        @block.gpsimd
        def _(pool):
            def settled():
                pool.sem_inc(pool_waits, 1)

            def rstd(dst, done, sums, width, at):
                src = sums[0]
                if len(sums) == 4:
                    nc.gpsimd.tensor_tensor(ss_pair[:, :, :], ss_v[:, 0:2, :], ss_v[:, 2:4, :],
                                            ALU.add).then_inc(pool_step, 1)
                    at = at + 1
                    pool.wait_ge(pool_step, at)
                    settled()
                    sums = (ss_pair[:, 0, :], ss_pair[:, 1, :])
                if len(sums) == 2:
                    nc.gpsimd.tensor_tensor(ss_sum[:, :], sums[0], sums[1], ALU.add).then_inc(pool_step, 1)
                    at = at + 1
                    pool.wait_ge(pool_step, at)
                    settled()
                    src = ss_sum[:, :]
                nc.gpsimd.tensor_scalar(mean[:, :], src, 1.0 / width, NORM_EPS, ALU.mult, ALU.add).then_inc(pool_step, 1)
                pool.wait_ge(pool_step, at + 1)
                settled()
                nc.gpsimd.tensor_tensor(dst[:, :], mean[:, :], minus_half[:, :], ALU.pow).then_inc(done, 1)

            def load_rows(dst, first, done):
                for c in range(CH):
                    pool.dma_start(dst[:, c, :], x[0, ds(first + c * P, P), :]).then_inc(done, 16)

            def scale_x():
                for c in range(CH):
                    nc.gpsimd.tensor_scalar(rows[:, c, :], rows[:, c, :], r_x[:, c:c + 1], None,
                                            ALU.mult).then_inc(x_scaled, 1)

            def history_of(b, i):
                pool.wait_ge(tapped, b * (8 * UNITS) + START + i * 8)
                pool.wait_ge(history_out, b * UNITS + START + i)
                settled()
                nc.gpsimd.tensor_copy(z[:, :, 0:2], history[:, ds(i, 1), :, :].rearrange("p a t n -> p (a t) n")
                                      ).then_inc(history_in, 1)
                pool.wait_ge(z_ready, b * UNITS + i + 1)
                pool.wait_ge(history_in, b * UNITS + i + 1)
                settled()
                nc.gpsimd.tensor_copy(history[:, ds(i, 1), :, :].rearrange("p a t n -> p (a t) n"),
                                      z[:, :, COLS:COLS + 2]).then_inc(history_out, 1)

            load_rows(rows, 0, x_loaded)
            load_rows(res, 0, res_loaded)
            nc.gpsimd.memset(ident[:, :], 0.0).then_inc(made, 1)
            pool.wait_ge(made, 3)
            nc.gpsimd.affine_select(out=ident[:, :], in_=ident[:, :], compare_op=ALU.not_equal, fill=1.0,
                                    base=0, pattern=[[-1, P]], channel_multiplier=1).then_inc(made, 1)
            pool.wait_ge(ws_loaded, 16)
            staged = staged_ws.rearrange("p (g s) -> p g s", g=GROUPS)
            nc.gpsimd.affine_select(out=staged, in_=staged, compare_op=ALU.is_ge, fill=0.0, base=0,
                                    pattern=[[0, GROUPS], [-1, P]], channel_multiplier=1).then_inc(made, 1)
            pool.sem_inc(history_out, START)
            pool.wait_ge(squared, CH)
            settled()
            rstd(r_x, r_x_ready, (ss_x[:, :],), D, 0)
            pool.wait_ge(r_x_ready, 1)
            settled()
            scale_x()
            with pool.Fori(0, BLOCKS) as b:
                step = b * STEP_BLOCK + STEP_FIRST
                pool.wait_ge(squared, b * SQ_BLOCK + SQ_FIRST + SQ_RES)
                settled()
                rstd(r_v, r_v_ready, (None,) * 4, AW, step + STEP_V)
                pool.wait_ge(squared, b * SQ_BLOCK + SQ_FIRST + SQ_X)
                settled()
                rstd(r_res, r_res_ready, (ss_res[:, 0, :], ss_res[:, 1, :]), D, step + STEP_RES)
                pool.wait_ge(transposed, b * T_BLOCK + T_FIRST + KT)
                settled()
                load_rows(rows, ((b + 1) % BLOCKS) * COLS, x_loaded)
                with pool.Fori(0, HALF_UNITS[0]) as i:
                    history_of(b, i)
                pool.wait_ge(squared, b * SQ_BLOCK + SQ_FIRST + SQ_OUT)
                settled()
                rstd(r_x, r_x_ready, (ss_x[:, :],), D, step + STEP_X)
                pool.wait_ge(r_x_ready, b + 2)
                settled()
                scale_x()
                with pool.Fori(HALF_UNITS[0], UNITS) as i:
                    history_of(b, i)
                pool.wait_ge(squared, (b + 1) * SQ_BLOCK + SQ_FIRST)
                settled()
                rstd(r_out, r_out_ready, (ss_out[:, :],), D, step + STEP_OUT)
                pool.wait_ge(r_out_ready, b + 1)
                settled()
                for c in range(CH):
                    nc.gpsimd.tensor_scalar(res[:, c, :], res[:, c, :], r_out[:, c:c + 1], None,
                                            ALU.mult).then_inc(pool_step, 1)
                    pool.wait_ge(pool_step, step + STEP_Y + c + 1)
                    settled()
                    nc.gpsimd.tensor_tensor(res[:, c, :], res[:, c, :], g_out[:, :], ALU.mult).then_inc(y_done, 1)
                    pool.wait_ge(y_done, b * CH + c + 1)
                    settled()
                    pool.dma_start(out[0, ds(b * COLS + c * P, P), :], res[:, c, :]).then_inc(y_stored, 16)
                pool.wait_ge(y_stored, (b + 1) * (16 * CH))
                settled()
                load_rows(res, ((b + 1) % BLOCKS) * COLS, res_loaded)
            pool.wait_ge(res_loaded, (BLOCKS + 1) * (16 * CH))
            settled()

        @block.tensor
        def _(pe):
            def part(pair, *at):
                return pair[0][at], pair[1][at]

            w, h, a = (w_hi, w_lo), (h_hi, h_lo), (a_hi, a_lo)
            everything = slice(None)

            def unit(b, mult, off, pairs, group, left, right, free, ready=None, after=None):
                for q in range(pairs):
                    pe.wait_ge(w_ready, b * PAIRS + RAW + mult + off + q + 1)
                    if ready is not None:
                        ready(q)
                    slot = (off + q) % SPLIT
                    for t in range(2):
                        k = 2 * q + t
                        for n in range(4):
                            if k == 0:
                                free(n)
                            last = product(ps[:, 4 * group + n, :], left(slot, t, k, n), right(slot, t, k, n),
                                           k == 0, k == 2 * pairs - 1)
                    last.then_inc(w_used, 1)
                    if after is not None:
                        after(q)

            def rows_out(left_tiles):
                return (lambda slot, t, k, n: part(left_tiles, everything, k, slice(n * P, (n + 1) * P)),
                        lambda slot, t, k, n: part(w, everything, slot, t, everything))

            def features_out(right_tiles):
                return (lambda slot, t, k, n: part(w, everything, slot, t, slice(n * P, (n + 1) * P)),
                        lambda slot, t, k, n: part(right_tiles, everything, k, everything))

            def turn(k, bank):
                for c in range(CH):
                    last = nc.tensor.transpose(ps[:, bank, c * P:(c + 1) * P], rows[:, c, k * P:(k + 1) * P],
                                               ident[:, :])
                last.then_inc(transposed, 1)

            def mix():
                for n in range(4):
                    for c in range(CH):
                        last = product(ps[:, 4 + n, c * P:(c + 1) * P],
                                       part(a, everything, VS + c, slice(n * P, (n + 1) * P)),
                                       part((ws_hi, ws_lo), everything, c, everything), True, True)
                last.then_inc(mix_done, 1)

            def product(out_ap, left, right, first, last):
                nc.tensor.matmul(out_ap, left[0], right[0], start=first, stop=False)
                nc.tensor.matmul(out_ap, left[0], right[1], start=False, stop=False)
                return nc.tensor.matmul(out_ap, left[1], right[0], start=False, stop=last)

            pe.sem_inc(w_used, SPLIT)
            pe.wait_ge(par_loaded, 16 * PARS)
            pe.wait_ge(made, 5)
            for i, n in enumerate((by_feature.shape[1], CONV_ROWS, CONV_ROWS)):
                last = nc.tensor.transpose(ps[:, 1, i * P:i * P + n], staged_par[0:n, i, :], ident[0:n, 0:n])
            last.then_inc(turned, 1)
            for g in range(GROUPS):
                last = nc.tensor.transpose(ps[:, 0, g * P:(g + 1) * P], staged_ws[:, g * P:(g + 1) * P], ident[:, :])
            last.then_inc(turned, 1)
            pe.wait_ge(set_up, 4)
            pe.wait_ge(x_scaled, CH)
            for k in range(KT):
                turn(k, k)
            with pe.Fori(0, BLOCKS) as b:
                def drained(nth):
                    pe.wait_ge(dve_drained, b * DV_BLOCK + T_FIRST + nth)

                def act_has_drained(nth):
                    pe.wait_ge(act_drained, b * AC_BLOCK + nth)

                with pe.Fori(0, 2) as gg:
                    for par in range(2):
                        unit(b, gg * (2 * Q), V_PAIR + Q * par, Q, par, *rows_out(h),
                             free=lambda n: drained(gg * 8 + 4 * (par - 2) + n + 1),
                             ready=lambda q: drained(0) if q == 2 else None)
                with pe.Fori(0, 2) as half:
                    mult = half * HALF_PAIRS
                    for g in range(2):
                        unit(b, mult, HALF_PAIR + Q * g, Q, 0, *features_out(h),
                             free=lambda n: act_has_drained(half * 8 + n + 1) if g else
                             drained(half * 16 + DV["v2"] + n + 1))
                        drained(half * 16 + (DV["m0"] if g else DV["v3"]) + 4)
                        pe.wait_ge(vs_ready, b * (4 * GROUPS) + half * 8 + 4 * g + 4)
                        pe.wait_ge(ws_ready, b * (4 * GROUPS) + half * 8 + 4 * g + 4)
                        mix()
                    for dh in range(2):
                        unit(b, mult, HALF_PAIR + Q * (2 + dh), Q, dh, *rows_out(a),
                             free=lambda n: drained(half * 16 + DV["m1"] + n + 1) if dh else
                             act_has_drained(half * 8 + 4 + n + 1),
                             ready=lambda q: pe.wait_ge(uv_ready, b * (4 * GROUPS) + half * 8 + START + 2 * q + 2))
                drained(DV["o11"] + 4)
                pe.wait_ge(res_scaled_dve, b * 2 + 2)
                pe.wait_ge(res_scaled_act, b * 2 + 2)
                for k in range(KT):
                    turn(k, k)
                for half in range(2):
                    base = sum(HALF_UNITS[:half])

                    def up_free(i, par, n):
                        drained(DV["d01" if par else "d00"] + n + 1 if half else DV["T2"] + 4 * par + n + 1)
                        act_has_drained(i * 4 + (AC_UP + 4 * (base - 2)) + n + 1)

                    def up_unit(i, mult, par, off):
                        unit(b, mult, off, Q, par, *features_out(h),
                             free=lambda n: up_free(i, par, n),
                             ready=(lambda q: drained(DV["T2"] + 2 * q + 2)) if half == 0 else None)

                    with pe.Fori(0, HALF_UNITS[half] // 2) as i2:
                        for par in range(2):
                            up_unit(i2 * 2 + par, i2 * (2 * Q), par, UP_PAIR[half] + Q * par)
                    if HALF_UNITS[half] % 2:
                        i = HALF_UNITS[half] - 1
                        up_unit(i, 0, i % 2, UP_PAIR[half] + Q * i)

                    def first_turns(q):
                        if q == 2:
                            act_has_drained(AC_UP + 4 * UNITS)
                            pe.wait_ge(x_scaled, b * CH + 2 * CH)
                            for k in range(4):
                                turn(k, k)

                    for dh in range(2):
                        unit(b, 0, DOWN_PAIR[half] + dh * HALF_UNITS[half], HALF_UNITS[half], (half + dh) % 2,
                             *rows_out(a),
                             free=lambda n: drained(DV["T1a"] + n + 1) if half and dh else
                             act_has_drained(AC_UP + 4 * (UNITS - 2 if half else HALF_UNITS[0] - 2 + dh) + n + 1),
                             ready=lambda q: pe.wait_ge(gv_ready, b * UNITS + START + base + q + 1),
                             after=first_turns if half and dh == 0 else None)
                drained(DV["d10"] + 4)
                for k in range(4, KT):
                    turn(k, k)


_INS = ['x', 'a_norm_g', 'a_w_in', 'a_b_in', 'a_v_norm_g', 'a_w_s', 'a_b_s', 'a_w_out',
        'ffn_norm_g', 'ffn_w_up', 'ffn_conv_w', 'ffn_conv_b', 'ffn_w_down', 'final_norm_g']


def kernel(**inputs):
    import numpy as _np
    import concourse.bacc as _bacc
    from concourse import mybir as _mybir
    from concourse.bass_utils import run_bass_kernel_spmd as _run

    nc = _bacc.Bacc("TRN2", target_bir_lowering=False, num_devices=1)
    arrays, args = {}, []
    for name in _INS:
        a = _np.ascontiguousarray(inputs[name])
        arrays[f"in_{name}_dram"] = a
        args.append(nc.dram_tensor(f"in_{name}_dram", a.shape, _mybir.dt.from_np(a.dtype), kind="ExternalInput").ap())
    out = nc.dram_tensor("out_0_dram", inputs['x'].shape, _mybir.dt.float32, kind="ExternalOutput").ap()
    gmlp_ffn_trunk(nc, *args, out)
    r = _run(nc, [arrays], core_ids=[0])
    return r.results[0]["out_0_dram"]
```

```python
import concourse.bass as bass
from concourse import mybir
from contextlib import ExitStack

P = 128
NORM_EPS = 1e-6


def gmlp_ffn_trunk(nc, x, a_norm_g, a_w_in, a_b_in, a_v_norm_g, a_w_s, a_b_s, a_w_out,
                   ffn_norm_g, ffn_w_up, ffn_conv_w, ffn_conv_b, ffn_w_down, final_norm_g, out):
    f32 = mybir.dt.float32
    f32r = mybir.dt.float32r
    ACT = mybir.ActivationFunctionType
    ALU = mybir.AluOpType
    ds = bass.ds

    SEQ, D = x.shape[1], x.shape[2]
    AW = a_w_out.shape[1]
    FW = ffn_w_down.shape[1]
    GROUPS = a_w_s.shape[1]
    COLS = 512
    CH = COLS // P
    BLOCKS = SEQ // COLS
    KT = D // P
    FT = FW // P
    UNITS = FT // 2
    HALF_UNITS = (6, 5)
    assert AW == GROUPS * COLS and KT == 8 and UNITS == sum(HALF_UNITS) and SEQ % COLS == 0

    Q = KT // 2
    V_PAIR = 0
    HALF_PAIR = 4 * Q
    HALF_PAIRS = 4 * Q
    UP_PAIR = (HALF_PAIR + 2 * HALF_PAIRS,)
    DOWN_PAIR = (UP_PAIR[0] + Q * HALF_UNITS[0],)
    UP_PAIR += (DOWN_PAIR[0] + 2 * HALF_UNITS[0],)
    DOWN_PAIR += (UP_PAIR[1] + Q * HALF_UNITS[1],)
    PAIRS = DOWN_PAIR[1] + 2 * HALF_UNITS[1]
    RAW = 4
    SPLIT = 2
    assert PAIRS % SPLIT == 0
    FILLS = [len(range(s, PAIRS, RAW)) for s in range(RAW)]

    END = {f"v{f}": V_PAIR + Q * (f + 1) for f in range(GROUPS)}
    for f in range(GROUPS):
        END[f"u{f}"] = HALF_PAIR + HALF_PAIRS * (f // 2) + Q * (f % 2 + 1)
    for half in range(2):
        for dh in range(2):
            END[f"o{half}{dh}"] = HALF_PAIR + HALF_PAIRS * half + Q * (3 + dh)
            END[f"d{half}{dh}"] = DOWN_PAIR[half] + HALF_UNITS[half] * (dh + 1)
    DV, n = {}, 0
    for name, banks in (("v0", 4), ("v1", 4), ("v2", 4), ("v3", 4), ("m0", 4), ("m1", 4), ("o00", 4),
                        ("o01", 4), ("m2", 4), ("m3", 4), ("o10", 4), ("o11", 4), ("T2", 8),
                        ("d00", 4), ("d01", 4), ("T1a", 4), ("d10", 4), ("d11", 4), ("T1b", 4)):
        DV[name] = n
        n += banks
    DV_BLOCK = n
    AC_UP = 4 * GROUPS
    AC_BLOCK = AC_UP + 4 * UNITS
    T_FIRST = KT
    T_BLOCK = 2 * KT

    ctx = ExitStack()
    with ctx:
        def sb(name, shape, dt=f32):
            return ctx.enter_context(nc.sbuf_tensor(name, shape, dt))

        def sem(name):
            return ctx.enter_context(nc.semaphore(name))

        w_raw = sb("w_raw", [P, RAW, 2, COLS])
        w_hi = sb("w_hi", [P, SPLIT, 2, COLS], f32r)
        w_lo = sb("w_lo", [P, SPLIT, 2, COLS], f32r)
        h_hi = sb("h_hi", [P, KT, COLS], f32r)
        h_lo = sb("h_lo", [P, KT, COLS], f32r)
        TILES = 2 * max(HALF_UNITS)
        a_hi = sb("a_hi", [P, TILES, COLS], f32r)
        a_lo = sb("a_lo", [P, TILES, COLS], f32r)
        VS = TILES - CH
        region = sb("region", [P, CH * AW + 8])
        v = region[:, 0:CH * AW].rearrange("p (c f) -> p c f", c=CH)
        rows = region[:, 0:CH * D].rearrange("p (c d) -> p c d", c=CH)
        conv = region[:, CH * D:CH * D + 4 * COLS].rearrange("p (t n) -> p t n", t=4)
        z = region[:, CH * D + 4 * COLS:CH * AW + 8].rearrange("p (t n) -> p t n", t=4)
        res = sb("res", [P, CH, D])
        u_gelu = sb("u_gelu", [P, 4, COLS])
        mixed = sb("mixed", [P, 2, COLS])
        squares = sb("squares", [P, D])
        ws_t = sb("ws_t", [P, GROUPS, P])
        ws_hi = sb("ws_hi", [P, CH, P], f32r)
        ws_lo = sb("ws_lo", [P, CH, P], f32r)
        history = sb("history", [P, UNITS, 4, 2])
        ident = sb("ident", [P, P])
        by_feature = sb("by_feature", [P, 2 * KT + 2 * (AW // P)])
        g_mix = by_feature[:, 0:KT]
        g_ffn = by_feature[:, KT:2 * KT]
        b_u = by_feature[:, 2 * KT:2 * KT + AW // P]
        g_v = by_feature[:, 2 * KT + AW // P:2 * KT + 2 * (AW // P)]
        conv_par = sb("conv_par", [P, 4, 2, FT])
        conv_w = conv_par[:, 0:3]
        conv_b = conv_par[:, 3]
        b_v = sb("b_v", [P, AW])
        b_s = sb("b_s", [P, GROUPS * P])
        g_out = sb("g_out", [P, D])
        ss_v = sb("ss_v", [P, GROUPS, CH])
        ss_res = sb("ss_res", [P, 2, CH])
        ss_x = sb("ss_x", [P, CH])
        ss_out = sb("ss_out", [P, 2, CH])
        ss_pair = sb("ss_pair", [P, 2, CH])
        ss_sum = sb("ss_sum", [P, CH])
        mean = sb("mean", [P, CH])
        minus_half = sb("minus_half", [P, CH])
        r_v = sb("r_v", [P, CH])
        r_res = sb("r_res", [P, CH])
        r_x = sb("r_x", [P, CH])
        r_out = sb("r_out", [P, CH])

        staged_ws = u_gelu[:, 0, :]
        staged_par = u_gelu[:, 1, 0:3 * P].rearrange("p (i n) -> p i n", i=3)
        CONV_ROWS = 2 * 2 * FT

        ps = ctx.enter_context(nc.psum_tensor("ps", [P, 8, COLS], f32))

        w_loaded = [sem(f"w_loaded{s}") for s in range(RAW)]
        w_hi_ready = sem("w_hi_ready")
        w_ready = sem("w_ready")
        w_used = sem("w_used")
        mix_done = sem("mix_done")
        bank_done = sem("bank_done")
        transposed = sem("transposed")
        dve_drained = sem("dve_drained")
        act_drained = sem("act_drained")
        h_hi_ready = sem("h_hi_ready")
        v_gelu = sem("v_gelu")
        vs_hi_ready = sem("vs_hi_ready")
        vs_ready = sem("vs_ready")
        ws_hi_ready = sem("ws_hi_ready")
        ws_ready = sem("ws_ready")
        uv_done = sem("uv_done")
        uv_hi_ready = sem("uv_hi_ready")
        uv_ready = sem("uv_ready")
        history_in = sem("history_in")
        z_ready = sem("z_ready")
        history_out = sem("history_out")
        tapped = sem("tapped")
        silu_done = sem("silu_done")
        gv_done = sem("gv_done")
        gv_hi_ready = sem("gv_hi_ready")
        gv_ready = sem("gv_ready")
        squared = sem("squared")
        r_v_ready = sem("r_v_ready")
        r_res_ready = sem("r_res_ready")
        r_x_ready = sem("r_x_ready")
        r_out_ready = sem("r_out_ready")
        x_scaled = sem("x_scaled")
        rows_scaled_dve = sem("rows_scaled_dve")
        rows_scaled_act = sem("rows_scaled_act")
        pool_step = sem("pool_step")
        pool_waits = sem("pool_waits")
        y_done = sem("y_done")
        y_tail = sem("y_tail")
        x_first = [sem(f"x_first{c}") for c in range(CH)]
        x_loaded = sem("x_loaded")
        res_loaded = sem("res_loaded")
        y_stored = sem("y_stored")
        y_stored_last = sem("y_stored_last")
        consts = sem("consts")
        par_loaded = sem("par_loaded")
        turned = sem("turned")
        set_up = sem("set_up")
        ws_loaded = sem("ws_loaded")
        made = sem("made")

        block = ctx.enter_context(nc.Block())

        SQ_V, SQ_RES, SQ_X, SQ_OUT = 0, 4 * GROUPS, 4 * GROUPS + 2 * CH, 4 * GROUPS + 3 * CH
        SQ_BLOCK = SQ_OUT + 2 * CH
        BD = {name: 3 * n for n, name in enumerate(("u0", "u1", "o01", "u2", "u3", "o11", "d11"))}
        BD_BLOCK = 3 * len(BD)
        SQ_FIRST = CH
        START = 1
        UV_START = 2
        CONSTS = 3
        PARS = 8

        STEP_V, STEP_RES, STEP_X, STEP_OUT, STEP_Y = 0, 3, 5, 6, 8
        STEP_BLOCK = STEP_Y + CH
        STEP_FIRST = 1

        @block.sync
        def _(sp):
            for c in range(CH):
                sp.dma_start(rows[:, c, :], x[0, c * P:(c + 1) * P, :]).then_inc(x_first[c], 16)

            def load(b, j, src, opens_block=False):
                slot = j[1] % RAW
                at = b * PAIRS + j[0] + j[1]
                if opens_block:
                    sp.wait_ge(w_ready, at + RAW - 1)
                else:
                    sp.wait_ge(w_ready, at + 1)
                for t in range(2):
                    sp.dma_start(w_raw[:, slot, t, :] if len(src[t].shape) == 2 else
                                 w_raw[:, slot, t, :].rearrange("p (h n) -> p h n", h=2),
                                 src[t]).then_inc(w_loaded[slot], 16)

            w_in, w_out = a_w_in[0], a_w_out[0]
            w_up = ffn_w_up[0].rearrange("k (h n) -> k h n", h=2)
            w_down = ffn_w_down[0]

            def in_tiles(q, col):
                return [w_in[(2 * q + t) * P:(2 * q + t + 1) * P, ds(col, COLS)] for t in range(2)]

            with sp.Fori(0, BLOCKS) as b:
                for f in range(GROUPS):
                    for q in range(Q):
                        load(b, (0, V_PAIR + Q * f + q), in_tiles(q, AW + f * COLS),
                             f == 0 and q < PAIRS % RAW)
                with sp.Fori(0, 2) as half:
                    first = half * HALF_PAIRS
                    for g in range(2):
                        for q in range(Q):
                            load(b, (first, HALF_PAIR + Q * g + q), in_tiles(q, half * (2 * COLS) + g * COLS))
                    for dh in range(2):
                        for q in range(Q):
                            row = half * (KT * P)
                            load(b, (first, HALF_PAIR + Q * (2 + dh) + q),
                                 [w_out[ds(row + (2 * q + t) * P, P), dh * COLS:(dh + 1) * COLS] for t in range(2)])
                for half in range(2):
                    base = sum(HALF_UNITS[:half])
                    with sp.Fori(0, HALF_UNITS[half]) as i:
                        for q in range(Q):
                            load(b, (i * Q, UP_PAIR[half] + q),
                                 [w_up[(2 * q + t) * P:(2 * q + t + 1) * P, :, ds(i * (2 * P) + base * 2 * P, 2 * P)]
                                  for t in range(2)])
                    for dh in range(2):
                        for i in range(HALF_UNITS[half]):
                            row = (base + i) * 2 * P
                            load(b, (0, DOWN_PAIR[half] + dh * HALF_UNITS[half] + i),
                                 [w_down[row + t * P:row + (t + 1) * P, dh * COLS:(dh + 1) * COLS] for t in range(2)])
            for q in range(SPLIT):
                load(BLOCKS, (0, q), in_tiles(q, AW), True)
            for c in range(CH):
                sp.wait_ge(y_tail, c + 1)
                sp.dma_start(out[0, (BLOCKS - 1) * COLS + c * P:(BLOCKS - 1) * COLS + (c + 1) * P, :],
                             res[:, c, :]).then_inc(y_stored_last, 16)
            sp.wait_ge(y_stored_last, 16 * CH)
            sp.wait_ge(y_stored, (BLOCKS - 1) * (16 * CH))

        @block.scalar
        def _(act):
            def split(b, mult, off):
                slot, half_slot = off % RAW, off % SPLIT
                if off >= PAIRS and isinstance(mult, int):
                    slot = off - PAIRS
                    fills = b * FILLS[slot] + FILLS[slot] + 1
                else:
                    fills = b * FILLS[slot] + mult // RAW + off // RAW + 1 if isinstance(mult, int) else \
                        b * FILLS[slot] + mult + off // RAW + 1
                    mult = mult if isinstance(mult, int) else mult * RAW
                act.wait_ge(w_loaded[slot], fills * 32)
                act.wait_ge(w_used, b * PAIRS + mult + off + 1)
                nc.scalar.activation(w_hi[:, half_slot], w_raw[:, slot], ACT.Copy).then_inc(w_hi_ready, 1)

            def square(b, nth, dst, src):
                if b is not None:
                    act.wait_ge(squared, b * SQ_BLOCK + SQ_FIRST + nth)
                elif nth:
                    act.wait_ge(squared, nth)
                nc.scalar.activation(squares[:, 0:src.shape[-1]], src, ACT.Square, accum_out=dst).then_inc(squared, 1)

            def scale_rows(src, r):
                for d in range(0, D, COLS):
                    for c in range(2, CH):
                        nc.scalar.activation(rows[:, c, d:d + COLS], src[:, c, d:d + COLS], ACT.Copy,
                                             scale=r[:, c:c + 1]).then_inc(rows_scaled_act, 1)

            def h_tile(bank, k, gain, nth):
                act.wait_ge(transposed, nth)
                nc.scalar.activation(h_hi[:, k, :], ps[:, bank, :], ACT.Copy,
                                     scale=gain[:, k:k + 1]).then_inc(h_hi_ready, 1)

            def v_drain(b, f, c):
                act.wait_ge(dve_drained, b * DV_BLOCK + T_FIRST + DV[f"v{f}"] + c + 1)
                tile = v[:, c, f * COLS:(f + 1) * COLS]
                nc.scalar.activation(tile, tile, ACT.Gelu_apprx_tanh).then_inc(v_gelu, 1)
                act.wait_ge(v_gelu, b * (4 * GROUPS) + 4 * f + c + 1)
                square(b, SQ_V + 4 * f + c, ss_v[:, f, c:c + 1], tile)

            def uv_hi(b, f, t):
                nth = 4 * f + t
                act.wait_ge(uv_done, b * (4 * GROUPS) + nth + 1)
                nc.scalar.activation(a_hi[:, 4 * (f % 2) + t, :], mixed[:, t % 2, :], ACT.Copy).then_inc(uv_hi_ready, 1)

            def ffn_z(b, i, par, end):
                act.wait_ge(w_used, b * PAIRS + SPLIT + end)
                act.wait_ge(history_in, b * UNITS + i + 1)
                nc.scalar.activation(z[:, :, 2:COLS + 2], ps[:, 4 * par:4 * par + 4, :], ACT.Copy).then_inc(z_ready, 1)
                act.wait_ge(gv_ready, b * UNITS + START + i)
                for t in range(2):
                    tap_last(i, par, t)

            def tap_last(i, par, t):
                tile = 2 * i + t % 2
                nc.scalar.activation(conv[:, t, :], ps[:, 4 * par + t, :], ACT.Identity,
                                     scale=conv_w[:, 2, t // 2, ds(tile, 1)],
                                     bias=conv_b[:, t // 2, ds(tile, 1)]).then_inc(act_drained, 1)

            def ffn_silu(b, i):
                act.wait_ge(tapped, b * (8 * UNITS) + START + i * 8 + 4)
                nc.scalar.activation(conv[:, 0:2, :], conv[:, 0:2, :], ACT.Silu).then_inc(silu_done, 1)

            def ffn_hi(b, i, tile):
                act.wait_ge(gv_done, b * UNITS + i + 1)
                nc.scalar.activation(a_hi[:, ds(tile, 2), :], conv[:, 0:2, :], ACT.Copy).then_inc(gv_hi_ready, 1)

            def ffn_piece(b, i, half, par, tile, q):
                if q == 0:
                    ffn_z(b, i, par, UP_PAIR[half] + Q * (i - sum(HALF_UNITS[:half]) + 1))
                elif q == 1:
                    for t in (2, 3):
                        tap_last(i, par, t)
                elif q == 2:
                    ffn_silu(b, i)
                elif q == 3:
                    ffn_hi(b, i, tile)

            row = 0
            for src in (a_norm_g[0], ffn_norm_g[0], a_b_in[0, 0:AW], a_v_norm_g[0]):
                tiles = src.rearrange("(k p) -> k p", p=P)
                act.dma_start(staged_par[row:row + tiles.shape[0], 0, :], tiles).then_inc(par_loaded, 16)
                row += tiles.shape[0]
            for i, src in enumerate((ffn_conv_w[0, 0], ffn_conv_w[0, 1], ffn_conv_w[0, 2], ffn_conv_b[0])):
                row = i % 2 * 2 * FT
                act.dma_start(staged_par[row:row + 2 * FT, 1 + i // 2, :],
                              src.rearrange("(k p) -> k p", p=P)).then_inc(par_loaded, 16)
            act.dma_start(staged_ws.rearrange("p (g s) -> p g s", g=GROUPS),
                          a_w_s[0].rearrange("g t s -> t g s")).then_inc(ws_loaded, 16)
            for c in range(CH):
                act.wait_ge(x_first[c], 16)
                square(None, c, ss_x[:, c:c + 1], rows[:, c, :])
            split(0, 0, 0)
            act.wait_ge(r_x_ready, 1)
            scale_rows(rows, r_x)
            split(0, 0, 1)
            act.wait_ge(set_up, 4)
            for k in range(KT):
                h_tile(k, k, g_mix, k + 1)

            with act.Fori(0, BLOCKS) as b:
                def drained(name, nth):
                    return b * DV_BLOCK + T_FIRST + DV[name] + nth

                for f in range(GROUPS):
                    for q in range(Q):
                        if f or q:
                            split(b, 0, V_PAIR + Q * f + q + 1)
                        if f:
                            v_drain(b, f - 1, q)
                for f in range(GROUPS):
                    half = f // 2
                    for q in range(Q):
                        split(b, 0, HALF_PAIR + HALF_PAIRS * half + Q * (f % 2) + q + 1)
                        if f == 0 and q < 2:
                            v_drain(b, GROUPS - 1, 2 * q)
                            v_drain(b, GROUPS - 1, 2 * q + 1)
                        elif f % 2:
                            uv_hi(b, f - 1, q)
                        if q in (1, 2):
                            if f and q == 1:
                                act.wait_ge(mix_done, b * (2 * GROUPS) + 2 * f)
                            for c in (2 * q - 2, 2 * q - 1):
                                act.wait_ge(v_gelu, b * (4 * GROUPS) + 4 * f + c + 1)
                                nc.scalar.activation(a_hi[:, VS + c, :], v[:, c, f * COLS:(f + 1) * COLS],
                                                     ACT.Copy).then_inc(vs_hi_ready, 1)
                        if q == 2:
                            act.wait_ge(r_v_ready, b + 1)
                            for c in range(CH):
                                nc.scalar.activation(ws_hi[:, c, :], ws_t[:, f, :], ACT.Copy,
                                                     scale=r_v[:, c:c + 1]).then_inc(ws_hi_ready, 1)
                    if f:
                        act.wait_ge(uv_done, b * (4 * GROUPS) + 4 * f)
                    for t in range(4):
                        if t < 3:
                            act.wait_ge(bank_done, b * BD_BLOCK + BD[f"u{f}"] + t + 1)
                        else:
                            act.wait_ge(w_used, b * PAIRS + SPLIT + END[f"u{f}"])
                        nc.scalar.activation(u_gelu[:, t, :], ps[:, t, :], ACT.Gelu_apprx_tanh,
                                             bias=b_u[:, 4 * f + t:4 * f + t + 1]).then_inc(act_drained, 1)
                    if f % 2:
                        for dh in range(2):
                            for q in range(Q):
                                split(b, 0, HALF_PAIR + HALF_PAIRS * half + Q * (2 + dh) + q + 1)
                                if dh == 0 and q < 2:
                                    uv_hi(b, f, 2 * q)
                                    uv_hi(b, f, 2 * q + 1)
                                if dh == 1 and half == 1:
                                    act.wait_ge(dve_drained, drained("o10", q + 1))
                                    square(b, SQ_RES + q, ss_res[:, 0, q:q + 1], res[:, q, 0:COLS])

                for c in range(CH):
                    act.wait_ge(dve_drained, drained("o11", c + 1))
                    square(b, SQ_RES + CH + c, ss_res[:, 1, c:c + 1], res[:, c, COLS:D])
                act.wait_ge(r_res_ready, b + 1)
                scale_rows(res, r_res)
                for k in range(KT):
                    h_tile(k, k, g_ffn, b * T_BLOCK + T_FIRST + k + 1)
                    if k == 3:
                        split(b, 0, UP_PAIR[0] + 1)

                for half in range(2):
                    base = sum(HALF_UNITS[:half])
                    for q in range(Q):
                        if half or q:
                            split(b, 0, UP_PAIR[half] + q + 1)
                    n_loops = (HALF_UNITS[half] - 1) // 2
                    with act.Fori(0, n_loops) as i2:
                        for par in range(2):
                            for q in range(Q):
                                split(b, i2 * 2, UP_PAIR[half] + Q * (par + 1) + q + 1)
                                ffn_piece(b, i2 * 2 + base + par, half, par, i2 * 4 + 2 * par, q)
                    if HALF_UNITS[half] % 2 == 0:
                        i = HALF_UNITS[half] - 2
                        for q in range(Q):
                            split(b, 0, UP_PAIR[half] + Q * (i + 1) + q + 1)
                            ffn_piece(b, base + i, half, i % 2, 2 * i, q)
                    i = HALF_UNITS[half] - 1
                    for dh in range(2):
                        for q in range(HALF_UNITS[half]):
                            split(b, 0, DOWN_PAIR[half] + dh * HALF_UNITS[half] + q + 1)
                            if dh == 0 and q < 4:
                                ffn_piece(b, base + i, half, i % 2, 2 * i, q)
                            if half and dh == 0 and q == 3:
                                for k in range(4):
                                    h_tile(k, k, g_mix, b * T_BLOCK + T_FIRST + KT + k + 1)
                            if half and dh == 1 and q < CH:
                                act.wait_ge(dve_drained, drained("d10", q + 1))
                                square(b, SQ_OUT + q, ss_out[:, 0, q:q + 1], res[:, q, 0:COLS])
                            if half == 0 and dh == 1 and q < CH:
                                if q == 0:
                                    act.wait_ge(x_loaded, (b + 1) * (16 * CH))
                                square(b, SQ_X + q, ss_x[:, q:q + 1], rows[:, q, :])
                for k in range(4, KT):
                    h_tile(k, k, g_mix, b * T_BLOCK + T_FIRST + KT + k + 1)
                split(b, 0, PAIRS + 1)
                for c in range(CH):
                    act.wait_ge(dve_drained, drained("d11", c + 1))
                    square(b, SQ_OUT + CH + c, ss_out[:, 1, c:c + 1], res[:, c, COLS:D])

        @block.vector
        def _(dve):
            def split(b, mult, off):
                dve.wait_ge(w_hi_ready, b * PAIRS + mult + off + 1)
                nc.vector.tensor_tensor(w_lo[:, off % SPLIT], w_raw[:, off % RAW if off < PAIRS else off - PAIRS],
                                        w_hi[:, off % SPLIT].bitcast(f32), ALU.subtract).then_inc(w_ready, 1)

            def h_tile(bank, k, gain, nth):
                dve.wait_ge(h_hi_ready, nth)
                nc.vector.scalar_tensor_tensor(out=h_lo[:, k, :], in0=ps[:, bank, :], scalar=gain[:, k:k + 1],
                                               in1=h_hi[:, k, :].bitcast(f32), op0=ALU.mult,
                                               op1=ALU.subtract).then_inc(dve_drained, 1)

            def scale_rows(src, r):
                for d in range(0, D, COLS):
                    for c in range(2):
                        nc.vector.tensor_scalar(rows[:, c, d:d + COLS], src[:, c, d:d + COLS], r[:, c:c + 1], None,
                                                ALU.mult).then_inc(rows_scaled_dve, 1)

            def v_bias(b, f, c):
                dve.wait_ge(w_used, b * PAIRS + SPLIT + END[f"v{f}"])
                if f == 0:
                    dve.wait_ge(history_out, b * UNITS + START)
                nc.vector.tensor_tensor(v[:, c, f * COLS:(f + 1) * COLS], ps[:, 4 * (f % 2) + c, :],
                                        b_v[:, f * COLS:(f + 1) * COLS], ALU.add).then_inc(dve_drained, 1)

            def uv(b, f, t):
                nth = b * (4 * GROUPS) + 4 * f + t
                dve.wait_ge(mix_done, b * (2 * GROUPS) + 2 * f + t // 2 + 1)
                dve.wait_ge(uv_ready, nth + UV_START - 1)
                nc.vector.scalar_tensor_tensor(
                    out=mixed[:, t % 2, :].rearrange("p (c t) -> p c t", c=CH),
                    in0=ps[:, 4 + t, :].rearrange("p (c t) -> p c t", c=CH),
                    scalar=g_v[:, 4 * f + t:4 * f + t + 1],
                    in1=b_s[:, f * P:(f + 1) * P].unsqueeze(1).to_broadcast([P, CH, P]),
                    op0=ALU.mult, op1=ALU.add).then_inc(dve_drained, 1)
                dve.wait_ge(dve_drained, b * DV_BLOCK + T_FIRST + DV[f"m{f}"] + t + 1)
                dve.wait_ge(act_drained, b * AC_BLOCK + 4 * f + t + 1)
                nc.vector.tensor_tensor(mixed[:, t % 2, :], mixed[:, t % 2, :], u_gelu[:, t, :],
                                        ALU.mult).then_inc(uv_done, 1)

            def uv_lo(b, f, t):
                dve.wait_ge(uv_hi_ready, b * (4 * GROUPS) + 4 * f + t + 1)
                nc.vector.tensor_tensor(a_lo[:, 4 * (f % 2) + t, :], mixed[:, t % 2, :],
                                        a_hi[:, 4 * (f % 2) + t, :].bitcast(f32), ALU.subtract).then_inc(uv_ready, 1)

            def add_res(b, name, par, dh, c):
                if name in BD and c < 3:
                    dve.wait_ge(bank_done, b * BD_BLOCK + BD[name] + c + 1)
                else:
                    dve.wait_ge(w_used, b * PAIRS + SPLIT + END[name])
                cols = res[:, c, dh * COLS:(dh + 1) * COLS]
                nc.vector.tensor_tensor(cols, cols, ps[:, 4 * par + c, :], ALU.add).then_inc(dve_drained, 1)

            def taps(b, i, pair):
                at = b * (8 * UNITS) + START + i * 8 + 4 * pair
                dve.wait_ge(z_ready, b * UNITS + i + 1)
                dve.wait_ge(act_drained, b * AC_BLOCK + AC_UP + i * 4 + 2 * pair + 2)
                for tap in (1, 0):
                    for t in (2 * pair, 2 * pair + 1):
                        if tap == 0:
                            dve.wait_ge(tapped, at + t % 2 + 1)
                        nc.vector.scalar_tensor_tensor(
                            out=conv[:, t, :], in0=z[:, t, tap:tap + COLS],
                            scalar=conv_w[:, tap, t // 2, ds(2 * i + t % 2, 1)], in1=conv[:, t, :],
                            op0=ALU.mult, op1=ALU.add).then_inc(tapped, 1)

            def ffn_piece(b, i, tile, q):
                if q == 1:
                    taps(b, i, 0)
                elif q == 2:
                    taps(b, i, 1)
                elif q == 3:
                    dve.wait_ge(silu_done, b * UNITS + i + 1)
                    dve.wait_ge(tapped, b * (8 * UNITS) + START + i * 8 + 8)
                    nc.vector.tensor_tensor(conv[:, 0:2, :], conv[:, 0:2, :], conv[:, 2:4, :],
                                            ALU.mult).then_inc(gv_done, 1)
                    dve.wait_ge(gv_hi_ready, b * UNITS + i + 1)
                    nc.vector.tensor_tensor(a_lo[:, ds(tile, 2), :], conv[:, 0:2, :],
                                            a_hi[:, ds(tile, 2), :].bitcast(f32), ALU.subtract).then_inc(gv_ready, 1)

            nc.vector.memset(minus_half[:, :], -0.5).then_inc(made, 1)
            nc.vector.memset(history[:, :, :, :], 0.0).then_inc(made, 1)
            dve.sem_inc(w_ready, RAW)
            dve.sem_inc(tapped, START)
            dve.sem_inc(gv_ready, START)
            dve.sem_inc(uv_ready, UV_START)
            dve.wait_ge(turned, 1)
            nc.vector.tensor_copy(by_feature[:, :], ps[:, 1, 0:by_feature.shape[1]]).then_inc(set_up, 1)
            for i in range(2):
                nc.vector.tensor_copy(conv_par[:, 2 * i:2 * i + 2].rearrange("p a h j -> p (a h j)"),
                                      ps[:, 1, (i + 1) * P:(i + 1) * P + CONV_ROWS]).then_inc(set_up, 1)
            dve.wait_ge(turned, 2)
            nc.vector.tensor_copy(ws_t[:, :, :], ps[:, 0, :].rearrange("p (g s) -> p g s", g=GROUPS)).then_inc(set_up, 1)
            dve.wait_ge(set_up, 4)
            split(0, 0, 0)
            dve.wait_ge(r_x_ready, 1)
            scale_rows(rows, r_x)
            split(0, 0, 1)
            for k in range(KT):
                h_tile(k, k, g_mix, k + 1)
            dve.wait_ge(consts, 16 * CONSTS)
            with dve.Fori(0, BLOCKS) as b:
                for f in range(GROUPS):
                    for q in range(Q):
                        if f or q:
                            split(b, 0, V_PAIR + Q * f + q + 1)
                        if f:
                            v_bias(b, f - 1, q)
                for f in range(GROUPS):
                    half = f // 2
                    for q in range(Q):
                        split(b, 0, HALF_PAIR + HALF_PAIRS * half + Q * (f % 2) + q + 1)
                        if f == 0 and q < 2:
                            v_bias(b, GROUPS - 1, 2 * q)
                            v_bias(b, GROUPS - 1, 2 * q + 1)
                        elif f % 2:
                            if q:
                                uv_lo(b, f - 1, q - 1)
                            uv(b, f - 1, q)
                        elif f:
                            add_res(b, "o01", 1, 1, q)
                        if q in (1, 2):
                            for c in (2 * q - 2, 2 * q - 1):
                                dve.wait_ge(vs_hi_ready, b * (4 * GROUPS) + 4 * f + c + 1)
                                nc.vector.tensor_tensor(a_lo[:, VS + c, :], v[:, c, f * COLS:(f + 1) * COLS],
                                                        a_hi[:, VS + c, :].bitcast(f32),
                                                        ALU.subtract).then_inc(vs_ready, 1)
                        if q == 2:
                            for c in range(CH):
                                dve.wait_ge(ws_hi_ready, b * (4 * GROUPS) + 4 * f + c + 1)
                                nc.vector.scalar_tensor_tensor(
                                    out=ws_lo[:, c, :], in0=ws_t[:, f, :], scalar=r_v[:, c:c + 1],
                                    in1=ws_hi[:, c, :].bitcast(f32), op0=ALU.mult,
                                    op1=ALU.subtract).then_inc(ws_ready, 1)
                    if f % 2:
                        uv_lo(b, f - 1, 3)
                        for dh in range(2):
                            for q in range(Q):
                                split(b, 0, HALF_PAIR + HALF_PAIRS * half + Q * (2 + dh) + q + 1)
                                if dh == 0 and q < 2:
                                    uv(b, f, 2 * q)
                                    uv(b, f, 2 * q + 1)
                                    uv_lo(b, f, 2 * q)
                                    uv_lo(b, f, 2 * q + 1)
                                if dh == 1:
                                    if half == 0 and q == 0:
                                        dve.wait_ge(res_loaded, (b + 1) * (16 * CH))
                                    add_res(b, f"o{half}0", 0, 0, q)
                for c in range(CH):
                    add_res(b, "o11", 1, 1, c)
                dve.wait_ge(r_res_ready, b + 1)
                scale_rows(res, r_res)
                for k in range(KT):
                    h_tile(k, k, g_ffn, b * T_BLOCK + T_FIRST + k + 1)
                    if k == 3:
                        split(b, 0, UP_PAIR[0] + 1)
                for half in range(2):
                    base = sum(HALF_UNITS[:half])
                    for q in range(Q):
                        if half or q:
                            split(b, 0, UP_PAIR[half] + q + 1)
                        if half:
                            add_res(b, "d01", 1, 1, q)
                    n_loops = (HALF_UNITS[half] - 1) // 2
                    with dve.Fori(0, n_loops) as i2:
                        for par in range(2):
                            for q in range(Q):
                                split(b, i2 * (2 * Q), UP_PAIR[half] + Q * (par + 1) + q + 1)
                                ffn_piece(b, i2 * 2 + base + par, i2 * 4 + 2 * par, q)
                    if HALF_UNITS[half] % 2 == 0:
                        i = HALF_UNITS[half] - 2
                        for q in range(Q):
                            split(b, 0, UP_PAIR[half] + Q * (i + 1) + q + 1)
                            ffn_piece(b, base + i, 2 * i, q)
                    i = HALF_UNITS[half] - 1
                    for dh in range(2):
                        for q in range(HALF_UNITS[half]):
                            split(b, 0, DOWN_PAIR[half] + dh * HALF_UNITS[half] + q + 1)
                            if dh == 0 and q < 4:
                                ffn_piece(b, base + i, 2 * i, q)
                            if half and dh == 0 and q == 3:
                                for k in range(4):
                                    h_tile(k, k, g_mix, b * T_BLOCK + T_FIRST + KT + k + 1)
                            if dh == 1 and q < CH:
                                add_res(b, f"d{half}0", half, 0, q)
                for c in range(CH):
                    add_res(b, "d11", 0, 1, c)
                for k in range(4, KT):
                    h_tile(k, k, g_mix, b * T_BLOCK + T_FIRST + KT + k + 1)
                split(b, 0, PAIRS + 1)
            dve.wait_ge(r_out_ready, BLOCKS)
            for c in range(CH):
                nc.vector.scalar_tensor_tensor(out=res[:, c, :], in0=res[:, c, :], scalar=r_out[:, c:c + 1],
                                               in1=g_out[:, :], op0=ALU.mult, op1=ALU.mult).then_inc(y_tail, 1)

        @block.gpsimd
        def _(pool):
            def settled():
                pool.sem_inc(pool_waits, 1)

            def rstd(dst, done, sums, width, at):
                src = sums[0]
                if len(sums) == 4:
                    nc.gpsimd.tensor_tensor(ss_pair[:, :, :], ss_v[:, 0:2, :], ss_v[:, 2:4, :],
                                            ALU.add).then_inc(pool_step, 1)
                    at = at + 1
                    pool.wait_ge(pool_step, at)
                    settled()
                    sums = (ss_pair[:, 0, :], ss_pair[:, 1, :])
                if len(sums) == 2:
                    nc.gpsimd.tensor_tensor(ss_sum[:, :], sums[0], sums[1], ALU.add).then_inc(pool_step, 1)
                    at = at + 1
                    pool.wait_ge(pool_step, at)
                    settled()
                    src = ss_sum[:, :]
                nc.gpsimd.tensor_scalar(mean[:, :], src, 1.0 / width, NORM_EPS, ALU.mult, ALU.add).then_inc(pool_step, 1)
                pool.wait_ge(pool_step, at + 1)
                settled()
                nc.gpsimd.tensor_tensor(dst[:, :], mean[:, :], minus_half[:, :], ALU.pow).then_inc(done, 1)

            def load_rows(dst, first, done):
                for c in range(CH):
                    pool.dma_start(dst[:, c, :], x[0, ds(first + c * P, P), :]).then_inc(done, 16)

            def scale_x():
                for c in range(CH):
                    nc.gpsimd.tensor_scalar(rows[:, c, :], rows[:, c, :], r_x[:, c:c + 1], None,
                                            ALU.mult).then_inc(x_scaled, 1)

            def history_of(b, i):
                pool.wait_ge(tapped, b * (8 * UNITS) + START + i * 8)
                pool.wait_ge(history_out, b * UNITS + START + i)
                settled()
                nc.gpsimd.tensor_copy(z[:, :, 0:2], history[:, ds(i, 1), :, :].rearrange("p a t n -> p (a t) n")
                                      ).then_inc(history_in, 1)
                pool.wait_ge(z_ready, b * UNITS + i + 1)
                pool.wait_ge(history_in, b * UNITS + i + 1)
                settled()
                nc.gpsimd.tensor_copy(history[:, ds(i, 1), :, :].rearrange("p a t n -> p (a t) n"),
                                      z[:, :, COLS:COLS + 2]).then_inc(history_out, 1)

            nc.gpsimd.memset(ident[:, :], 0.0).then_inc(made, 1)
            pool.wait_ge(made, 3)
            nc.gpsimd.affine_select(out=ident[:, :], in_=ident[:, :], compare_op=ALU.not_equal, fill=1.0,
                                    base=0, pattern=[[-1, P]], channel_multiplier=1).then_inc(made, 1)
            pool.wait_ge(ws_loaded, 16)
            staged = staged_ws.rearrange("p (g s) -> p g s", g=GROUPS)
            nc.gpsimd.affine_select(out=staged, in_=staged, compare_op=ALU.is_ge, fill=0.0, base=0,
                                    pattern=[[0, GROUPS], [-1, P]], channel_multiplier=1).then_inc(made, 1)
            for dst, src in ((b_v, a_b_in[0, AW:2 * AW]), (b_s, a_b_s[0].rearrange("g t -> (g t)")),
                             (g_out, final_norm_g)):
                pool.dma_start(dst[:, :], src.partition_broadcast(P)).then_inc(consts, 16)
            load_rows(res, 0, res_loaded)
            pool.sem_inc(history_out, START)
            pool.wait_ge(squared, CH)
            rstd(r_x, r_x_ready, (ss_x[:, :],), D, 0)

            def block_norms(b, last):
                step = b * STEP_BLOCK + STEP_FIRST
                pool.wait_ge(squared, b * SQ_BLOCK + SQ_FIRST + SQ_RES)
                rstd(r_v, r_v_ready, (None,) * 4, AW, step + STEP_V)
                pool.wait_ge(squared, b * SQ_BLOCK + SQ_FIRST + SQ_X)
                rstd(r_res, r_res_ready, (ss_res[:, 0, :], ss_res[:, 1, :]), D, step + STEP_RES)
                pool.wait_ge(transposed, b * T_BLOCK + T_FIRST + KT)
                settled()
                load_rows(rows, b * COLS if last else (b + 1) * COLS, x_loaded)
                with pool.Fori(0, HALF_UNITS[0]) as i:
                    history_of(b, i)
                pool.wait_ge(squared, b * SQ_BLOCK + SQ_FIRST + SQ_OUT)
                settled()
                rstd(r_x, r_x_ready, (ss_x[:, :],), D, step + STEP_X)
                pool.wait_ge(r_x_ready, b + 2)
                settled()
                scale_x()
                with pool.Fori(HALF_UNITS[0], UNITS) as i:
                    history_of(b, i)
                pool.wait_ge(squared, (b + 1) * SQ_BLOCK + SQ_FIRST)
                rstd(r_out, r_out_ready, (ss_out[:, 0, :], ss_out[:, 1, :]), D, step + STEP_OUT)
                if last:
                    return
                pool.wait_ge(r_out_ready, b + 1)
                settled()
                for c in range(CH):
                    nc.gpsimd.tensor_scalar(res[:, c, :], res[:, c, :], r_out[:, c:c + 1], None,
                                            ALU.mult).then_inc(pool_step, 1)
                    pool.wait_ge(pool_step, step + STEP_Y + c + 1)
                    settled()
                    nc.gpsimd.tensor_tensor(res[:, c, :], res[:, c, :], g_out[:, :], ALU.mult).then_inc(y_done, 1)
                    pool.wait_ge(y_done, b * CH + c + 1)
                    settled()
                    pool.dma_start(out[0, ds(b * COLS + c * P, P), :], res[:, c, :]).then_inc(y_stored, 16)
                pool.wait_ge(y_stored, (b + 1) * (16 * CH))
                settled()
                load_rows(res, (b + 1) * COLS, res_loaded)

            with pool.Fori(0, BLOCKS - 1) as b:
                block_norms(b, False)
            block_norms(BLOCKS - 1, True)

        @block.tensor
        def _(pe):
            def part(pair, *at):
                return pair[0][at], pair[1][at]

            w, h, a = (w_hi, w_lo), (h_hi, h_lo), (a_hi, a_lo)
            everything = slice(None)

            def unit(b, mult, off, pairs, group, left, right, free, ready=None, after=None, beside=None,
                     by_bank=False):
                for q in range(pairs):
                    pe.wait_ge(w_ready, b * PAIRS + RAW + mult + off + q + 1)
                    if ready is not None:
                        ready(q)
                    slot = (off + q) % SPLIT
                    final = q == pairs - 1
                    order = [(t, n) for t in range(2) for n in range(4)]
                    if by_bank and final:
                        order = [(t, n) for n in range(4) for t in range(2)]
                    for i, (t, n) in enumerate(order):
                        k = 2 * q + t
                        if k == 0:
                            free(n)
                        last = product(ps[:, 4 * group + n, :], left(slot, t, k, n), right(slot, t, k, n),
                                       k == 0, k == 2 * pairs - 1,
                                       beside, q, 3 * i)
                        if by_bank and final and t == 1 and n < 3:
                            last.then_inc(bank_done, 1)
                    last.then_inc(w_used, 1)
                    if after is not None:
                        after(q)

            def rows_out(left_tiles):
                return (lambda slot, t, k, n: part(left_tiles, everything, k, slice(n * P, (n + 1) * P)),
                        lambda slot, t, k, n: part(w, everything, slot, t, everything))

            def features_out(right_tiles):
                return (lambda slot, t, k, n: part(w, everything, slot, t, slice(n * P, (n + 1) * P)),
                        lambda slot, t, k, n: part(right_tiles, everything, k, everything))

            def turn(k, bank):
                for c in range(CH):
                    last = nc.tensor.transpose(ps[:, bank, c * P:(c + 1) * P], rows[:, c, k * P:(k + 1) * P],
                                               ident[:, :])
                last.then_inc(transposed, 1)

            def mix_pass(j, bank_free):
                n, c, which = j // (3 * CH), j // 3 % CH, j % 3
                if j % (3 * CH) == 0:
                    bank_free(n)
                left, right = (a_hi, a_hi, a_lo)[which], (ws_hi, ws_lo, ws_hi)[which]
                last = nc.tensor.matmul(ps[:, 4 + n, c * P:(c + 1) * P], left[:, VS + c, n * P:(n + 1) * P],
                                        right[:, c, :], start=which == 0, stop=which == 2)
                if j % (6 * CH) == 6 * CH - 1:
                    last.then_inc(mix_done, 1)

            def product(out_ap, left, right, first, last, beside, q, i):
                for j, (l, r) in enumerate(((0, 0), (0, 1), (1, 0))):
                    if beside is not None:
                        beside(q, i + j)
                    mm = nc.tensor.matmul(out_ap, left[l], right[r], start=first and j == 0, stop=last and j == 2)
                return mm

            pe.sem_inc(w_used, SPLIT)
            pe.wait_ge(par_loaded, 16 * PARS)
            pe.wait_ge(made, 5)
            for i, n in enumerate((by_feature.shape[1], CONV_ROWS, CONV_ROWS)):
                last = nc.tensor.transpose(ps[:, 1, i * P:i * P + n], staged_par[0:n, i, :], ident[0:n, 0:n])
            last.then_inc(turned, 1)
            for g in range(GROUPS):
                last = nc.tensor.transpose(ps[:, 0, g * P:(g + 1) * P], staged_ws[:, g * P:(g + 1) * P], ident[:, :])
            last.then_inc(turned, 1)
            pe.wait_ge(set_up, 4)
            for k in range(KT):
                if k % 4 == 0:
                    pe.wait_ge(rows_scaled_dve, k // 2 + 2)
                    pe.wait_ge(rows_scaled_act, k // 2 + 2)
                turn(k, k)
            with pe.Fori(0, BLOCKS) as b:
                def drained(nth):
                    pe.wait_ge(dve_drained, b * DV_BLOCK + T_FIRST + nth)

                def act_has_drained(nth):
                    pe.wait_ge(act_drained, b * AC_BLOCK + nth)

                with pe.Fori(0, 2) as gg:
                    for par in range(2):
                        unit(b, gg * (2 * Q), V_PAIR + Q * par, Q, par, *rows_out(h),
                             free=lambda n: drained(gg * 8 + 4 * (par - 2) + n + 1),
                             ready=lambda q: drained(0) if q == 2 else None)
                with pe.Fori(0, 2) as half:
                    mult = half * HALF_PAIRS

                    def mix_free(g, n):
                        drained(half * 16 + (DV["m0"] if g else DV["v3"]) + n + 1)

                    def beside_u(g, q, i):
                        if q == Q - 1:
                            mix_pass(i, lambda n: mix_free(g, n))
                        if g and q == 0:
                            mix_pass(6 * CH + i, lambda n: mix_free(0, n))

                    for g in range(2):
                        def mix_ready(q):
                            if q == Q - 1:
                                pe.wait_ge(vs_ready, b * (4 * GROUPS) + half * 8 + 4 * g + 4)
                                pe.wait_ge(ws_ready, b * (4 * GROUPS) + half * 8 + 4 * g + 4)

                        unit(b, mult, HALF_PAIR + Q * g, Q, 0, *features_out(h),
                             free=lambda n: act_has_drained(half * 8 + n + 1) if g else
                             drained(half * 16 + DV["v2"] + n + 1),
                             ready=mix_ready, beside=lambda q, i: beside_u(g, q, i), by_bank=True)
                    for dh in range(2):
                        unit(b, mult, HALF_PAIR + Q * (2 + dh), Q, dh, *rows_out(a),
                             free=lambda n: drained(half * 16 + DV["m1"] + n + 1) if dh else
                             act_has_drained(half * 8 + 4 + n + 1),
                             ready=lambda q: pe.wait_ge(uv_ready, b * (4 * GROUPS) + half * 8 + UV_START + 2 * q + 2),
                             beside=None if dh else
                             lambda q, i: mix_pass(6 * CH + i, lambda n: mix_free(1, n)) if q == 0 else None,
                             by_bank=bool(dh))
                drained(DV["o11"] + 4)
                for k in range(KT):
                    if k % 4 == 0:
                        pe.wait_ge(rows_scaled_dve, b * 4 + 4 + k // 2 + 2)
                        pe.wait_ge(rows_scaled_act, b * 4 + 4 + k // 2 + 2)
                    turn(k, k)
                for half in range(2):
                    base = sum(HALF_UNITS[:half])

                    def up_free(i, par, n):
                        drained(DV["d01" if par else "d00"] + n + 1 if half else DV["T2"] + 4 * par + n + 1)
                        act_has_drained(i * 4 + (AC_UP + 4 * (base - 2)) + n + 1)

                    def up_unit(i, mult, par, off):
                        unit(b, mult, off, Q, par, *features_out(h),
                             free=lambda n: up_free(i, par, n),
                             ready=(lambda q: drained(DV["T2"] + 2 * q + 2)) if half == 0 else None)

                    with pe.Fori(0, HALF_UNITS[half] // 2) as i2:
                        for par in range(2):
                            up_unit(i2 * 2 + par, i2 * (2 * Q), par, UP_PAIR[half] + Q * par)
                    if HALF_UNITS[half] % 2:
                        i = HALF_UNITS[half] - 1
                        up_unit(i, 0, i % 2, UP_PAIR[half] + Q * i)

                    def first_turns(q):
                        if q == 2:
                            act_has_drained(AC_UP + 4 * UNITS)
                            pe.wait_ge(x_scaled, b * CH + CH)
                            for k in range(4):
                                turn(k, k)

                    for dh in range(2):
                        unit(b, 0, DOWN_PAIR[half] + dh * HALF_UNITS[half], HALF_UNITS[half], (half + dh) % 2,
                             *rows_out(a),
                             free=lambda n: drained(DV["T1a"] + n + 1) if half and dh else
                             act_has_drained(AC_UP + 4 * (UNITS - 2 if half else HALF_UNITS[0] - 2 + dh) + n + 1),
                             ready=lambda q: pe.wait_ge(gv_ready, b * UNITS + START + base + q + 1),
                             after=first_turns if half and dh == 0 else None, by_bank=bool(half and dh))
                drained(DV["d10"] + 4)
                for k in range(4, KT):
                    turn(k, k)


_INS = ['x', 'a_norm_g', 'a_w_in', 'a_b_in', 'a_v_norm_g', 'a_w_s', 'a_b_s', 'a_w_out',
        'ffn_norm_g', 'ffn_w_up', 'ffn_conv_w', 'ffn_conv_b', 'ffn_w_down', 'final_norm_g']


def kernel(**inputs):
    import numpy as _np
    import concourse.bacc as _bacc
    from concourse import mybir as _mybir
    from concourse.bass_utils import run_bass_kernel_spmd as _run

    nc = _bacc.Bacc("TRN2", target_bir_lowering=False, num_devices=1)
    arrays, args = {}, []
    for name in _INS:
        a = _np.ascontiguousarray(inputs[name])
        arrays[f"in_{name}_dram"] = a
        args.append(nc.dram_tensor(f"in_{name}_dram", a.shape, _mybir.dt.from_np(a.dtype), kind="ExternalInput").ap())
    out = nc.dram_tensor("out_0_dram", inputs['x'].shape, _mybir.dt.float32, kind="ExternalOutput").ap()
    gmlp_ffn_trunk(nc, *args, out)
    r = _run(nc, [arrays], core_ids=[0])
    return r.results[0]["out_0_dram"]
```

```python
import concourse.bass as bass
from concourse import mybir
from contextlib import ExitStack

P = 128
NORM_EPS = 1e-6


def gmlp_ffn_trunk(nc, x, a_norm_g, a_w_in, a_b_in, a_v_norm_g, a_w_s, a_b_s, a_w_out,
                   ffn_norm_g, ffn_w_up, ffn_conv_w, ffn_conv_b, ffn_w_down, final_norm_g, out):
    f32 = mybir.dt.float32
    f32r = mybir.dt.float32r
    ACT = mybir.ActivationFunctionType
    ALU = mybir.AluOpType
    ds = bass.ds

    SEQ, D = x.shape[1], x.shape[2]
    AW = a_w_out.shape[1]
    FW = ffn_w_down.shape[1]
    GROUPS = a_w_s.shape[1]
    COLS = 512
    CH = COLS // P
    BLOCKS = SEQ // COLS
    KT = D // P
    FT = FW // P
    UNITS = FT // 2
    HALF_UNITS = (6, 5)
    assert AW == GROUPS * COLS and KT == 8 and UNITS == sum(HALF_UNITS) and SEQ % COLS == 0

    Q = KT // 2
    V_PAIR = 0
    HALF_PAIR = 4 * Q
    HALF_PAIRS = 4 * Q
    UP_PAIR = (HALF_PAIR + 2 * HALF_PAIRS,)
    DOWN_PAIR = (UP_PAIR[0] + Q * HALF_UNITS[0],)
    UP_PAIR += (DOWN_PAIR[0] + 2 * HALF_UNITS[0],)
    DOWN_PAIR += (UP_PAIR[1] + Q * HALF_UNITS[1],)
    PAIRS = DOWN_PAIR[1] + 2 * HALF_UNITS[1]
    RAW = 4
    SPLIT = 2
    assert PAIRS % SPLIT == 0
    FILLS = [len(range(s, PAIRS, RAW)) for s in range(RAW)]

    END = {f"v{f}": V_PAIR + Q * (f + 1) for f in range(GROUPS)}
    for f in range(GROUPS):
        END[f"u{f}"] = HALF_PAIR + HALF_PAIRS * (f // 2) + Q * (f % 2 + 1)
    for half in range(2):
        for dh in range(2):
            END[f"o{half}{dh}"] = HALF_PAIR + HALF_PAIRS * half + Q * (3 + dh)
            END[f"d{half}{dh}"] = DOWN_PAIR[half] + HALF_UNITS[half] * (dh + 1)
    DV, n = {}, 0
    for name, banks in (("v0", 4), ("v1", 4), ("v2", 4), ("v3", 4), ("m0", 4), ("m1", 4), ("o00", 4),
                        ("o01", 4), ("m2", 4), ("m3", 4), ("o10", 4), ("o11", 4), ("T2", 8),
                        ("d00", 4), ("d01", 4), ("T1a", 4), ("d10", 4), ("d11", 4), ("T1b", 4)):
        DV[name] = n
        n += banks
    DV_BLOCK = n
    AC_UP = 4 * GROUPS
    AC_BLOCK = AC_UP + 4 * UNITS
    T_FIRST = KT
    T_BLOCK = 2 * KT

    ctx = ExitStack()
    with ctx:
        def sb(name, shape, dt=f32):
            return ctx.enter_context(nc.sbuf_tensor(name, shape, dt))

        def sem(name):
            return ctx.enter_context(nc.semaphore(name))

        w_raw = sb("w_raw", [P, RAW, 2, COLS])
        w_hi = sb("w_hi", [P, SPLIT, 2, COLS], f32r)
        w_lo = sb("w_lo", [P, SPLIT, 2, COLS], f32r)
        h_hi = sb("h_hi", [P, KT, COLS], f32r)
        h_lo = sb("h_lo", [P, KT, COLS], f32r)
        TILES = 2 * max(HALF_UNITS)
        a_hi = sb("a_hi", [P, TILES, COLS], f32r)
        a_lo = sb("a_lo", [P, TILES, COLS], f32r)
        VS = TILES - CH
        region = sb("region", [P, CH * AW + 8])
        v = region[:, 0:CH * AW].rearrange("p (c f) -> p c f", c=CH)
        rows = region[:, 0:CH * D].rearrange("p (c d) -> p c d", c=CH)
        conv = region[:, CH * D:CH * D + 4 * COLS].rearrange("p (t n) -> p t n", t=4)
        z = region[:, CH * D + 4 * COLS:CH * AW + 8].rearrange("p (t n) -> p t n", t=4)
        res = sb("res", [P, CH, D])
        u_gelu = sb("u_gelu", [P, 4, COLS])
        mixed = sb("mixed", [P, 2, COLS])
        squares = sb("squares", [P, D])
        ws_t = sb("ws_t", [P, GROUPS, P])
        ws_split = sb("ws_split", [P, CH, 2, P], f32r)
        history = sb("history", [P, UNITS, 4, 2])
        ident = sb("ident", [P, P])
        by_feature = sb("by_feature", [P, 2 * KT + 2 * (AW // P)])
        g_mix = by_feature[:, 0:KT]
        g_ffn = by_feature[:, KT:2 * KT]
        b_u = by_feature[:, 2 * KT:2 * KT + AW // P]
        g_v = by_feature[:, 2 * KT + AW // P:2 * KT + 2 * (AW // P)]
        conv_par = sb("conv_par", [P, 4, 2, FT])
        conv_w = conv_par[:, 0:3]
        conv_b = conv_par[:, 3]
        b_v = sb("b_v", [P, AW])
        b_s = sb("b_s", [P, GROUPS * P])
        g_out = sb("g_out", [P, D])
        ss_v = sb("ss_v", [P, GROUPS, CH])
        ss_res = sb("ss_res", [P, 2, CH])
        ss_x = sb("ss_x", [P, CH])
        ss_out = sb("ss_out", [P, 2, CH])
        ss_pair = sb("ss_pair", [P, 2, CH])
        ss_sum = sb("ss_sum", [P, CH])
        mean = sb("mean", [P, CH])
        minus_half = sb("minus_half", [P, CH])
        r_v = sb("r_v", [P, CH])
        r_res = sb("r_res", [P, CH])
        r_x = sb("r_x", [P, CH])
        r_out = sb("r_out", [P, CH])

        staged_ws = u_gelu[:, 0, :]
        staged_par = u_gelu[:, 1, 0:3 * P].rearrange("p (i n) -> p i n", i=3)
        CONV_ROWS = 2 * 2 * FT

        ps = ctx.enter_context(nc.psum_tensor("ps", [P, 8, COLS], f32))

        w_loaded = [sem(f"w_loaded{s}") for s in range(RAW)]
        w_hi_ready = sem("w_hi_ready")
        w_ready = sem("w_ready")
        w_used = sem("w_used")
        mix_done = sem("mix_done")
        mix_half = sem("mix_half")
        bank_done = sem("bank_done")
        transposed = sem("transposed")
        dve_drained = sem("dve_drained")
        act_drained = sem("act_drained")
        h_hi_ready = sem("h_hi_ready")
        v_gelu = sem("v_gelu")
        vs_hi_ready = sem("vs_hi_ready")
        vs_ready = sem("vs_ready")
        ws_hi_ready = sem("ws_hi_ready")
        ws_ready = sem("ws_ready")
        uv_done = sem("uv_done")
        uv_hi_ready = sem("uv_hi_ready")
        uv_ready = sem("uv_ready")
        history_in = sem("history_in")
        z_ready = sem("z_ready")
        history_out = sem("history_out")
        tapped = sem("tapped")
        silu_done = sem("silu_done")
        gv_done = sem("gv_done")
        gv_hi_ready = sem("gv_hi_ready")
        gv_ready = sem("gv_ready")
        squared = sem("squared")
        norm_step = sem("norm_step")
        mean_ready = sem("mean_ready")
        r_v_ready = sem("r_v_ready")
        r_res_ready = sem("r_res_ready")
        r_x_ready = sem("r_x_ready")
        r_out_ready = sem("r_out_ready")
        x_scaled = sem("x_scaled")
        rows_scaled_dve = sem("rows_scaled_dve")
        rows_scaled_act = sem("rows_scaled_act")
        y_scaled = sem("y_scaled")
        y_done = sem("y_done")
        y_tail = sem("y_tail")
        pool_waits = sem("pool_waits")
        x_first = [sem(f"x_first{c}") for c in range(CH)]
        x_loaded = sem("x_loaded")
        res_loaded = sem("res_loaded")
        y_stored = sem("y_stored")
        y_stored_last = sem("y_stored_last")
        consts = sem("consts")
        par_loaded = sem("par_loaded")
        ws_loaded = sem("ws_loaded")
        made = sem("made")
        turned = sem("turned")
        set_up = sem("set_up")
        table_loaded = sem("table_loaded")

        block = ctx.enter_context(nc.Block())

        SQ_V, SQ_RES, SQ_X, SQ_OUT = 0, 4 * GROUPS, 4 * GROUPS + 2 * CH, 4 * GROUPS + 3 * CH
        SQ_BLOCK = SQ_OUT + 2 * CH
        BD = {name: 3 * n for n, name in enumerate(("u0", "u1", "o01", "u2", "u3", "o11", "d11"))}
        BD_BLOCK = 3 * len(BD)
        SQ_FIRST = CH
        START = 1
        UV_START = 2
        CONSTS = 3
        WARMING = 10
        PARS = 8

        NORM_V, NORM_RES, NORM_OUT, NORM_BLOCK = 0, 2, 4, 6
        MEAN_V, MEAN_RES, MEAN_X, MEAN_OUT, MEAN_BLOCK = 1, 2, 4, 5, 6

        @block.sync
        def _(sp):
            for c in range(CH):
                sp.dma_start(rows[:, c, :], x[0, c * P:(c + 1) * P, :]).then_inc(x_first[c], 16)

            def load(b, j, src, opens_block=False):
                slot = j[1] % RAW
                at = b * PAIRS + j[0] + j[1]
                if opens_block:
                    sp.wait_ge(w_ready, at + RAW - 1)
                else:
                    sp.wait_ge(w_ready, at + 1)
                for t in range(2):
                    sp.dma_start(w_raw[:, slot, t, :] if len(src[t].shape) == 2 else
                                 w_raw[:, slot, t, :].rearrange("p (h n) -> p h n", h=2),
                                 src[t]).then_inc(w_loaded[slot], 16)

            w_in, w_out = a_w_in[0], a_w_out[0]
            w_up = ffn_w_up[0].rearrange("k (h n) -> k h n", h=2)
            w_down = ffn_w_down[0]

            def in_tiles(q, col):
                return [w_in[(2 * q + t) * P:(2 * q + t + 1) * P, ds(col, COLS)] for t in range(2)]

            with sp.Fori(0, BLOCKS) as b:
                for f in range(GROUPS):
                    for q in range(Q):
                        load(b, (0, V_PAIR + Q * f + q), in_tiles(q, AW + f * COLS),
                             f == 0 and q < PAIRS % RAW)
                with sp.Fori(0, 2) as half:
                    first = half * HALF_PAIRS
                    for g in range(2):
                        for q in range(Q):
                            load(b, (first, HALF_PAIR + Q * g + q), in_tiles(q, half * (2 * COLS) + g * COLS))
                    for dh in range(2):
                        for q in range(Q):
                            row = half * (KT * P)
                            load(b, (first, HALF_PAIR + Q * (2 + dh) + q),
                                 [w_out[ds(row + (2 * q + t) * P, P), dh * COLS:(dh + 1) * COLS] for t in range(2)])
                for half in range(2):
                    base = sum(HALF_UNITS[:half])
                    with sp.Fori(0, HALF_UNITS[half]) as i:
                        for q in range(Q):
                            load(b, (i * Q, UP_PAIR[half] + q),
                                 [w_up[(2 * q + t) * P:(2 * q + t + 1) * P, :, ds(i * (2 * P) + base * 2 * P, 2 * P)]
                                  for t in range(2)])
                    for dh in range(2):
                        for i in range(HALF_UNITS[half]):
                            row = (base + i) * 2 * P
                            load(b, (0, DOWN_PAIR[half] + dh * HALF_UNITS[half] + i),
                                 [w_down[row + t * P:row + (t + 1) * P, dh * COLS:(dh + 1) * COLS] for t in range(2)])
            load(BLOCKS, (0, 0), in_tiles(0, AW), True)
            for c in range(CH):
                sp.wait_ge(y_tail, c + 1)
                sp.dma_start(out[0, (BLOCKS - 1) * COLS + c * P:(BLOCKS - 1) * COLS + (c + 1) * P, :],
                             res[:, c, :]).then_inc(y_stored_last, 16)
            sp.wait_ge(y_stored_last, 16 * CH)
            sp.wait_ge(y_stored, (BLOCKS - 1) * (16 * CH))

        @block.scalar
        def _(act):
            def split(b, mult, off):
                slot, half_slot = off % RAW, off % SPLIT
                if off >= PAIRS and isinstance(mult, int):
                    slot = off - PAIRS
                    fills = b * FILLS[slot] + FILLS[slot] + 1
                else:
                    fills = b * FILLS[slot] + mult // RAW + off // RAW + 1 if isinstance(mult, int) else \
                        b * FILLS[slot] + mult + off // RAW + 1
                    mult = mult if isinstance(mult, int) else mult * RAW
                act.wait_ge(w_loaded[slot], fills * 32)
                act.wait_ge(w_used, b * PAIRS + mult + off + 1)
                nc.scalar.activation(w_hi[:, half_slot], w_raw[:, slot], ACT.Copy).then_inc(w_hi_ready, 1)

            def square(b, nth, dst, src):
                if b is not None:
                    act.wait_ge(squared, b * SQ_BLOCK + SQ_FIRST + nth)
                elif nth:
                    act.wait_ge(squared, nth)
                nc.scalar.activation(squares[:, 0:src.shape[-1]], src, ACT.Square, accum_out=dst).then_inc(squared, 1)

            def scale_rows(src, r, wait_pair=None):
                for c, d in ((1, 0), (1, COLS), (3, COLS)):
                    if wait_pair is not None and c == 3:
                        wait_pair()
                    nc.scalar.activation(rows[:, c, d:d + COLS], src[:, c, d:d + COLS], ACT.Copy,
                                         scale=r[:, c:c + 1]).then_inc(rows_scaled_act, 1)

            def h_tile(bank, k, gain, nth):
                act.wait_ge(transposed, nth)
                nc.scalar.activation(h_hi[:, k, :], ps[:, bank, :], ACT.Copy,
                                     scale=gain[:, k:k + 1]).then_inc(h_hi_ready, 1)

            def v_drain(b, f, c):
                act.wait_ge(dve_drained, b * DV_BLOCK + T_FIRST + DV[f"v{f}"] + c + 1)
                tile = v[:, c, f * COLS:(f + 1) * COLS]
                nc.scalar.activation(tile, tile, ACT.Gelu_apprx_tanh).then_inc(v_gelu, 1)
                act.wait_ge(v_gelu, b * (4 * GROUPS) + 4 * f + c + 1)
                square(b, SQ_V + 4 * f + c, ss_v[:, f, c:c + 1], tile)

            def uv_hi(b, f, t):
                nth = 4 * f + t
                act.wait_ge(uv_done, b * (4 * GROUPS) + nth + 1)
                nc.scalar.activation(a_hi[:, 4 * (f % 2) + t, :], mixed[:, t % 2, :],
                                     ACT.Copy).then_inc(uv_hi_ready, 1)

            def ffn_z(b, i, par, end):
                act.wait_ge(w_used, b * PAIRS + SPLIT + end)
                act.wait_ge(history_in, b * UNITS + i + 1)
                nc.scalar.activation(z[:, :, 2:COLS + 2], ps[:, 4 * par:4 * par + 4, :], ACT.Copy).then_inc(z_ready, 1)
                act.wait_ge(gv_ready, b * UNITS + START + i)
                for t in range(2):
                    tap_last(i, par, t)

            def tap_last(i, par, t):
                tile = 2 * i + t % 2
                nc.scalar.activation(conv[:, t, :], ps[:, 4 * par + t, :], ACT.Identity,
                                     scale=conv_w[:, 2, t // 2, ds(tile, 1)],
                                     bias=conv_b[:, t // 2, ds(tile, 1)]).then_inc(act_drained, 1)

            def ffn_silu(b, i):
                act.wait_ge(tapped, b * (8 * UNITS) + START + i * 8 + 4)
                nc.scalar.activation(conv[:, 0:2, :], conv[:, 0:2, :], ACT.Silu).then_inc(silu_done, 1)

            def ffn_hi(b, i, tile):
                act.wait_ge(gv_done, b * UNITS + i + 1)
                nc.scalar.activation(a_hi[:, ds(tile, 2), :], conv[:, 0:2, :], ACT.Copy).then_inc(gv_hi_ready, 1)

            def ffn_piece(b, i, half, par, tile, q):
                if q == 0:
                    ffn_z(b, i, par, UP_PAIR[half] + Q * (i - sum(HALF_UNITS[:half]) + 1))
                elif q == 1:
                    for t in (2, 3):
                        tap_last(i, par, t)
                elif q == 2:
                    ffn_silu(b, i)
                elif q == 3:
                    ffn_hi(b, i, tile)

            row = 0
            for src in (a_norm_g[0], ffn_norm_g[0], a_b_in[0, 0:AW], a_v_norm_g[0]):
                tiles = src.rearrange("(k p) -> k p", p=P)
                act.dma_start(staged_par[row:row + tiles.shape[0], 0, :], tiles).then_inc(par_loaded, 16)
                row += tiles.shape[0]
            for i, src in enumerate((ffn_conv_w[0, 0], ffn_conv_w[0, 1], ffn_conv_w[0, 2], ffn_conv_b[0])):
                row = i % 2 * 2 * FT
                act.dma_start(staged_par[row:row + 2 * FT, 1 + i // 2, :],
                              src.rearrange("(k p) -> k p", p=P)).then_inc(par_loaded, 16)
            act.dma_start(staged_ws.rearrange("p (g s) -> p g s", g=GROUPS),
                          a_w_s[0].rearrange("g t s -> t g s")).then_inc(ws_loaded, 16)
            act.wait_ge(made, 3)
            nc.scalar.activation(squares[:, 0:1], minus_half[:, 0:1], ACT.Square).then_inc(table_loaded, 1)
            act.wait_ge(table_loaded, 1)
            for c in range(CH):
                act.wait_ge(x_first[c], 16)
                square(None, c, ss_x[:, c:c + 1], rows[:, c, :])
            split(0, 0, 0)
            act.wait_ge(r_x_ready, 1)
            scale_rows(rows, r_x)
            act.wait_ge(set_up, 4)
            for k in range(4):
                h_tile(k, k, g_mix, k + 1)

            with act.Fori(0, BLOCKS) as b:
                def drained(name, nth):
                    return b * DV_BLOCK + T_FIRST + DV[name] + nth

                for f in range(GROUPS):
                    for q in range(Q):
                        split(b, 0, V_PAIR + Q * f + q + 1)
                        if f == 0 and q == 0:
                            for k in range(4, KT):
                                h_tile(k, k, g_mix, b * T_BLOCK + k + 1)
                        if f:
                            v_drain(b, f - 1, q)
                for f in range(GROUPS):
                    half = f // 2
                    for q in range(Q):
                        split(b, 0, HALF_PAIR + HALF_PAIRS * half + Q * (f % 2) + q + 1)
                        if f and q == 1:
                            act.wait_ge(mix_done, b * (4 * GROUPS) + 4 * f)
                        if (f == 0 and q < 2) or q == 1:
                            for c in range(CH) if f else (2 * q, 2 * q + 1):
                                act.wait_ge(v_gelu, b * (4 * GROUPS) + 4 * f + c + 1)
                                nc.scalar.activation(a_hi[:, VS + c, :], v[:, c, f * COLS:(f + 1) * COLS],
                                                     ACT.Copy).then_inc(vs_hi_ready, 1)
                        if f == 0 and q < 2:
                            v_drain(b, GROUPS - 1, 2 * q)
                            v_drain(b, GROUPS - 1, 2 * q + 1)
                        if q == 2:
                            act.wait_ge(r_v_ready, b + 1)
                            for c in range(CH):
                                nc.scalar.activation(ws_split[:, c, 0, :], ws_t[:, f, :], ACT.Copy,
                                                     scale=r_v[:, c:c + 1]).then_inc(ws_hi_ready, 1)
                        if f % 2:
                            for t in ((0, 1), (), (2, 3), ())[q]:
                                uv_hi(b, f - 1, t)
                    if f:
                        act.wait_ge(uv_done, b * (4 * GROUPS) + 4 * f)
                    for t in range(4):
                        if t < 3:
                            act.wait_ge(bank_done, b * BD_BLOCK + BD[f"u{f}"] + t + 1)
                        else:
                            act.wait_ge(w_used, b * PAIRS + SPLIT + END[f"u{f}"])
                        nc.scalar.activation(u_gelu[:, t, :], ps[:, t, :], ACT.Gelu_apprx_tanh,
                                             bias=b_u[:, 4 * f + t:4 * f + t + 1]).then_inc(act_drained, 1)
                    if f % 2:
                        for dh in range(2):
                            for q in range(Q):
                                split(b, 0, HALF_PAIR + HALF_PAIRS * half + Q * (2 + dh) + q + 1)
                                if dh == 0 and q < 2:
                                    uv_hi(b, f, 2 * q)
                                    uv_hi(b, f, 2 * q + 1)
                                if dh == 1 and half == 1 and q < 2:
                                    for c in (2 * q, 2 * q + 1):
                                        act.wait_ge(dve_drained, drained("o10", c + 1))
                                        square(b, SQ_RES + c, ss_res[:, 0, c:c + 1], res[:, c, 0:COLS])

                for c in range(CH):
                    act.wait_ge(dve_drained, drained("o11", c + 1))
                    square(b, SQ_RES + CH + c, ss_res[:, 1, c:c + 1], res[:, c, COLS:D])
                act.wait_ge(r_res_ready, b * 2 + 1)
                scale_rows(res, r_res, lambda: act.wait_ge(r_res_ready, b * 2 + 2))
                for k in range(KT):
                    h_tile(k, k, g_ffn, b * T_BLOCK + T_FIRST + k + 1)
                    if k == 3:
                        split(b, 0, UP_PAIR[0] + 1)

                for half in range(2):
                    base = sum(HALF_UNITS[:half])
                    for q in range(Q):
                        if half or q:
                            split(b, 0, UP_PAIR[half] + q + 1)
                    n_loops = (HALF_UNITS[half] - 1) // 2
                    with act.Fori(0, n_loops) as i2:
                        for par in range(2):
                            for q in range(Q):
                                split(b, i2 * 2, UP_PAIR[half] + Q * (par + 1) + q + 1)
                                ffn_piece(b, i2 * 2 + base + par, half, par, i2 * 4 + 2 * par, q)
                    if HALF_UNITS[half] % 2 == 0:
                        i = HALF_UNITS[half] - 2
                        for q in range(Q):
                            split(b, 0, UP_PAIR[half] + Q * (i + 1) + q + 1)
                            ffn_piece(b, base + i, half, i % 2, 2 * i, q)
                    i = HALF_UNITS[half] - 1
                    for dh in range(2):
                        for q in range(HALF_UNITS[half]):
                            split(b, 0, DOWN_PAIR[half] + dh * HALF_UNITS[half] + q + 1)
                            if dh == 0 and q < 4:
                                ffn_piece(b, base + i, half, i % 2, 2 * i, q)
                            if half and dh == 0 and q == 3:
                                for k in range(4):
                                    h_tile(k, k, g_mix, b * T_BLOCK + T_FIRST + KT + k + 1)
                            if half and dh == 1 and q < CH:
                                act.wait_ge(dve_drained, drained("d10", q + 1))
                                square(b, SQ_OUT + q, ss_out[:, 0, q:q + 1], res[:, q, 0:COLS])
                            if half == 0 and dh == 1 and q < CH:
                                if q == 0:
                                    act.wait_ge(x_loaded, (b + 1) * (16 * CH))
                                square(b, SQ_X + q, ss_x[:, q:q + 1], rows[:, q, :])
                for c in range(CH):
                    act.wait_ge(dve_drained, drained("d11", c + 1))
                    square(b, SQ_OUT + CH + c, ss_out[:, 1, c:c + 1], res[:, c, COLS:D])

        @block.vector
        def _(dve):
            def split(b, mult, off):
                dve.wait_ge(w_hi_ready, b * PAIRS + mult + off + 1)
                nc.vector.tensor_tensor(w_lo[:, off % SPLIT], w_raw[:, off % RAW if off < PAIRS else off - PAIRS],
                                        w_hi[:, off % SPLIT].bitcast(f32), ALU.subtract).then_inc(w_ready, 1)

            def h_tile(bank, k, gain, nth):
                dve.wait_ge(h_hi_ready, nth)
                nc.vector.scalar_tensor_tensor(out=h_lo[:, k, :], in0=ps[:, bank, :], scalar=gain[:, k:k + 1],
                                               in1=h_hi[:, k, :].bitcast(f32), op0=ALU.mult,
                                               op1=ALU.subtract).then_inc(dve_drained, 1)

            def scale_rows(src, r, between=None):
                for c, d in ((0, 0), (0, COLS), (2, 0), (2, COLS), (3, 0)):
                    if between is not None and (c, d) == (2, 0):
                        between()
                    nc.vector.tensor_scalar(rows[:, c, d:d + COLS], src[:, c, d:d + COLS], r[:, c:c + 1], None,
                                            ALU.mult).then_inc(rows_scaled_dve, 1)

            def mean_of(cs, sums, width, at):
                src = sums[0]
                if len(sums) == 4:
                    nc.vector.tensor_tensor(ss_pair[:, :, :], ss_v[:, 0:2, :], ss_v[:, 2:4, :],
                                            ALU.add).then_inc(norm_step, 1)
                    at = at + 1
                    dve.wait_ge(norm_step, at)
                    sums = (ss_pair[:, 0, :], ss_pair[:, 1, :])
                if len(sums) == 2:
                    nc.vector.tensor_tensor(ss_sum[:, cs], sums[0], sums[1], ALU.add).then_inc(norm_step, 1)
                    dve.wait_ge(norm_step, at + 1)
                    src = ss_sum[:, cs]
                nc.vector.tensor_scalar(mean[:, cs], src, 1.0 / width, NORM_EPS, ALU.mult,
                                        ALU.add).then_inc(mean_ready, 1)

            def mean_of_pair(b, pair, squares_at, sums, at):
                dve.wait_ge(squared, b * SQ_BLOCK + SQ_FIRST + squares_at + CH + 2 * pair + 2)
                cs = slice(2 * pair, 2 * pair + 2)
                mean_of(cs, (sums[:, 0, cs], sums[:, 1, cs]), D, b * NORM_BLOCK + at + pair)

            def v_bias(b, f, c):
                dve.wait_ge(w_used, b * PAIRS + SPLIT + END[f"v{f}"])
                if f == 0:
                    dve.wait_ge(history_out, b * UNITS + START)
                nc.vector.tensor_tensor(v[:, c, f * COLS:(f + 1) * COLS], ps[:, 4 * (f % 2) + c, :],
                                        b_v[:, f * COLS:(f + 1) * COLS], ALU.add).then_inc(dve_drained, 1)

            def mix_drain(b, f, t):
                nth = b * (4 * GROUPS) + 4 * f + t
                dve.wait_ge(mix_done, nth + 1)
                dve.wait_ge(uv_ready, nth + UV_START - 1)
                parts = ps[:, 4 + 2 * (t % 2):6 + 2 * (t % 2), :].rearrange("p k (c h n) -> p (k c) h n", c=2, h=2)
                into = mixed[:, t % 2, :].rearrange("p (c n) -> p c n", c=CH)
                gain = g_v[:, 4 * f + t:4 * f + t + 1]
                nc.vector.scalar_tensor_tensor(
                    out=into, in0=parts[:, :, 0, :], scalar=gain,
                    in1=b_s[:, f * P:(f + 1) * P].unsqueeze(1).to_broadcast([P, CH, P]),
                    op0=ALU.mult, op1=ALU.add).then_inc(mix_half, 1)
                dve.wait_ge(mix_half, nth + 1)
                nc.vector.scalar_tensor_tensor(
                    out=into, in0=parts[:, :, 1, :], scalar=gain, in1=into,
                    op0=ALU.mult, op1=ALU.add).then_inc(dve_drained, 1)

            def uv(b, f, t):
                dve.wait_ge(dve_drained, b * DV_BLOCK + T_FIRST + DV[f"m{f}"] + t + 1)
                dve.wait_ge(act_drained, b * AC_BLOCK + 4 * f + t + 1)
                nc.vector.tensor_tensor(mixed[:, t % 2, :], mixed[:, t % 2, :], u_gelu[:, t, :],
                                        ALU.mult).then_inc(uv_done, 1)

            def uv_lo(b, f, t):
                dve.wait_ge(uv_hi_ready, b * (4 * GROUPS) + 4 * f + t + 1)
                nc.vector.tensor_tensor(a_lo[:, 4 * (f % 2) + t, :], mixed[:, t % 2, :],
                                        a_hi[:, 4 * (f % 2) + t, :].bitcast(f32), ALU.subtract).then_inc(uv_ready, 1)

            def u_beside(b, f, q):
                if q == 0:
                    for t in (0, 1):
                        uv(b, f, t)
                    for t in (0, 1):
                        uv_lo(b, f, t)
                elif q == 1:
                    mix_drain(b, f, 2)
                    uv(b, f, 2)
                    mix_drain(b, f, 3)
                elif q == 2:
                    uv(b, f, 3)
                    for t in (2, 3):
                        uv_lo(b, f, t)

            def add_res(b, name, par, dh, c):
                if name in BD and c < 3:
                    dve.wait_ge(bank_done, b * BD_BLOCK + BD[name] + c + 1)
                else:
                    dve.wait_ge(w_used, b * PAIRS + SPLIT + END[name])
                cols = res[:, c, dh * COLS:(dh + 1) * COLS]
                nc.vector.tensor_tensor(cols, cols, ps[:, 4 * par + c, :], ALU.add).then_inc(dve_drained, 1)

            def taps(b, i, pair):
                at = b * (8 * UNITS) + START + i * 8 + 4 * pair
                dve.wait_ge(z_ready, b * UNITS + i + 1)
                dve.wait_ge(act_drained, b * AC_BLOCK + AC_UP + i * 4 + 2 * pair + 2)
                for tap in (1, 0):
                    for t in (2 * pair, 2 * pair + 1):
                        if tap == 0:
                            dve.wait_ge(tapped, at + t % 2 + 1)
                        nc.vector.scalar_tensor_tensor(
                            out=conv[:, t, :], in0=z[:, t, tap:tap + COLS],
                            scalar=conv_w[:, tap, t // 2, ds(2 * i + t % 2, 1)], in1=conv[:, t, :],
                            op0=ALU.mult, op1=ALU.add).then_inc(tapped, 1)

            def ffn_piece(b, i, tile, q):
                if q == 1:
                    taps(b, i, 0)
                elif q == 2:
                    taps(b, i, 1)
                elif q == 3:
                    dve.wait_ge(silu_done, b * UNITS + i + 1)
                    dve.wait_ge(tapped, b * (8 * UNITS) + START + i * 8 + 8)
                    nc.vector.tensor_tensor(conv[:, 0:2, :], conv[:, 0:2, :], conv[:, 2:4, :],
                                            ALU.mult).then_inc(gv_done, 1)
                    dve.wait_ge(gv_hi_ready, b * UNITS + i + 1)
                    nc.vector.tensor_tensor(a_lo[:, ds(tile, 2), :], conv[:, 0:2, :],
                                            a_hi[:, ds(tile, 2), :].bitcast(f32), ALU.subtract).then_inc(gv_ready, 1)

            nc.vector.memset(minus_half[:, :], -0.5).then_inc(made, 1)
            nc.vector.memset(history[:, :, :, :], 0.0).then_inc(made, 1)
            dve.sem_inc(w_ready, RAW)
            dve.sem_inc(tapped, START)
            dve.sem_inc(gv_ready, START)
            dve.sem_inc(uv_ready, UV_START)
            dve.wait_ge(squared, CH)
            mean_of(slice(0, CH), (ss_x[:, :],), D, 0)
            dve.wait_ge(turned, 1)
            nc.vector.tensor_copy(by_feature[:, :], ps[:, 1, 0:by_feature.shape[1]]).then_inc(set_up, 1)
            for i in range(2):
                nc.vector.tensor_copy(conv_par[:, 2 * i:2 * i + 2].rearrange("p a h j -> p (a h j)"),
                                      ps[:, 1, (i + 1) * P:(i + 1) * P + CONV_ROWS]).then_inc(set_up, 1)
            dve.wait_ge(turned, 2)
            nc.vector.tensor_copy(ws_t[:, :, :], ps[:, 0, :].rearrange("p (g s) -> p g s", g=GROUPS)).then_inc(set_up, 1)
            dve.wait_ge(set_up, 4)
            dve.wait_ge(r_x_ready, 1)
            scale_rows(rows, r_x)
            split(0, 0, 0)
            for k in range(4):
                h_tile(k, k, g_mix, k + 1)
            dve.wait_ge(consts, 16 * CONSTS)
            dve.sem_inc(r_out_ready, START)
            with dve.Fori(0, BLOCKS) as b:
                for f in range(GROUPS):
                    for q in range(Q):
                        split(b, 0, V_PAIR + Q * f + q + 1)
                        if f == 0 and q == 0:
                            for k in range(4, KT):
                                h_tile(k, k, g_mix, b * T_BLOCK + k + 1)
                        if f:
                            v_bias(b, f - 1, q)
                for f in range(GROUPS):
                    half = f // 2
                    for q in range(Q):
                        split(b, 0, HALF_PAIR + HALF_PAIRS * half + Q * (f % 2) + q + 1)
                        if f == 0 and q < 2:
                            v_bias(b, GROUPS - 1, 2 * q)
                            v_bias(b, GROUPS - 1, 2 * q + 1)
                        if (f == 0 and q < 2) or q == 1:
                            for c in range(CH) if f else (2 * q, 2 * q + 1):
                                dve.wait_ge(vs_hi_ready, b * (4 * GROUPS) + 4 * f + c + 1)
                                nc.vector.tensor_tensor(a_lo[:, VS + c, :], v[:, c, f * COLS:(f + 1) * COLS],
                                                        a_hi[:, VS + c, :].bitcast(f32),
                                                        ALU.subtract).then_inc(vs_ready, 1)
                        if f == 0 and q == 1:
                            dve.wait_ge(squared, b * SQ_BLOCK + SQ_FIRST + SQ_RES)
                            dve.wait_ge(r_out_ready, b * 2 + START)
                            mean_of(slice(0, CH), (None,) * 4, AW, b * NORM_BLOCK + NORM_V)
                        if q == 2:
                            if f == 0:
                                dve.wait_ge(r_v_ready, b + 1)
                            for c in range(CH):
                                dve.wait_ge(ws_hi_ready, b * (4 * GROUPS) + 4 * f + c + 1)
                                nc.vector.scalar_tensor_tensor(
                                    out=ws_split[:, c, 1, :], in0=ws_t[:, f, :], scalar=r_v[:, c:c + 1],
                                    in1=ws_split[:, c, 0, :].bitcast(f32), op0=ALU.mult,
                                    op1=ALU.subtract).then_inc(ws_ready, 1)
                        if f % 2:
                            u_beside(b, f - 1, q)
                        elif f and q < 2:
                            add_res(b, "o01", 1, 1, 2 * q)
                            add_res(b, "o01", 1, 1, 2 * q + 1)
                    for t in range(2):
                        mix_drain(b, f, t)
                    if f % 2:
                        for dh in range(2):
                            for q in range(Q):
                                if not (half and dh and q == Q - 1):
                                    split(b, 0, HALF_PAIR + HALF_PAIRS * half + Q * (2 + dh) + q + 1)
                                if dh == 0 and q < 2:
                                    for t in (2 * q, 2 * q + 1):
                                        if q:
                                            mix_drain(b, f, t)
                                        uv(b, f, t)
                                    uv_lo(b, f, 2 * q)
                                    uv_lo(b, f, 2 * q + 1)
                                if dh == 1 and q < 2:
                                    if half == 0 and q == 0:
                                        dve.wait_ge(res_loaded, (b + 1) * (16 * CH))
                                    add_res(b, f"o{half}0", 0, 0, 2 * q)
                                    add_res(b, f"o{half}0", 0, 0, 2 * q + 1)
                for c in range(CH):
                    if c == 3:
                        mean_of_pair(b, 0, SQ_RES, ss_res, NORM_RES)
                    add_res(b, "o11", 1, 1, c)

                def last_chunks():
                    mean_of_pair(b, 1, SQ_RES, ss_res, NORM_RES)
                    dve.wait_ge(r_res_ready, b * 2 + 2)

                dve.wait_ge(r_res_ready, b * 2 + 1)
                scale_rows(res, r_res, last_chunks)
                split(b, 0, UP_PAIR[0])
                for k in range(KT):
                    h_tile(k, k, g_ffn, b * T_BLOCK + T_FIRST + k + 1)
                    if k == 3:
                        split(b, 0, UP_PAIR[0] + 1)
                for half in range(2):
                    base = sum(HALF_UNITS[:half])
                    for q in range(Q):
                        if half or q:
                            split(b, 0, UP_PAIR[half] + q + 1)
                        if half:
                            add_res(b, "d01", 1, 1, q)
                    n_loops = (HALF_UNITS[half] - 1) // 2
                    with dve.Fori(0, n_loops) as i2:
                        for par in range(2):
                            for q in range(Q):
                                split(b, i2 * (2 * Q), UP_PAIR[half] + Q * (par + 1) + q + 1)
                                ffn_piece(b, i2 * 2 + base + par, i2 * 4 + 2 * par, q)
                    if HALF_UNITS[half] % 2 == 0:
                        i = HALF_UNITS[half] - 2
                        for q in range(Q):
                            split(b, 0, UP_PAIR[half] + Q * (i + 1) + q + 1)
                            ffn_piece(b, base + i, 2 * i, q)
                    i = HALF_UNITS[half] - 1
                    for dh in range(2):
                        for q in range(HALF_UNITS[half]):
                            split(b, 0, DOWN_PAIR[half] + dh * HALF_UNITS[half] + q + 1)
                            if dh == 0 and q < 4:
                                ffn_piece(b, base + i, 2 * i, q)
                            if half and dh == 0 and q == 3:
                                for k in range(4):
                                    h_tile(k, k, g_mix, b * T_BLOCK + T_FIRST + KT + k + 1)
                            if dh == 1 and q < CH:
                                add_res(b, f"d{half}0", half, 0, q)
                            if half == 0 and dh == 1 and q == HALF_UNITS[0] - 1:
                                dve.wait_ge(squared, b * SQ_BLOCK + SQ_FIRST + SQ_OUT)
                                mean_of(slice(0, CH), (ss_x[:, :],), D, 0)
                dve.wait_ge(r_x_ready, b + 2)
                for c in range(CH):
                    if c == 3:
                        mean_of_pair(b, 0, SQ_OUT, ss_out, NORM_OUT)
                    add_res(b, "d11", 0, 1, c)
                mean_of_pair(b, 1, SQ_OUT, ss_out, NORM_OUT)
            for c in range(CH):
                if c % 2 == 0:
                    dve.wait_ge(r_out_ready, BLOCKS * 2 + START + c // 2 - 1)
                nc.vector.scalar_tensor_tensor(out=res[:, c, :], in0=res[:, c, :], scalar=r_out[:, c:c + 1],
                                               in1=g_out[:, :], op0=ALU.mult, op1=ALU.mult).then_inc(y_tail, 1)

        @block.gpsimd
        def _(pool):
            def settled():
                pool.sem_inc(pool_waits, 1)

            everyone = slice(0, CH)

            def root(dst, done, cs, nth):
                pool.wait_ge(mean_ready, nth)
                nc.gpsimd.tensor_tensor(dst[:, cs], mean[:, cs], minus_half[:, cs], ALU.pow).then_inc(done, 1)

            def load_rows(dst, first, done):
                for c in range(CH):
                    pool.dma_start(dst[:, c, :], x[0, ds(first + c * P, P), :]).then_inc(done, 16)

            def scale_x():
                for c in range(CH):
                    nc.gpsimd.tensor_scalar(rows[:, c, :], rows[:, c, :], r_x[:, c:c + 1], None,
                                            ALU.mult).then_inc(x_scaled, 1)

            def history_of(b, i):
                pool.wait_ge(tapped, b * (8 * UNITS) + START + i * 8)
                pool.wait_ge(history_out, b * UNITS + START + i)
                settled()
                nc.gpsimd.tensor_copy(z[:, :, 0:2], history[:, ds(i, 1), :, :].rearrange("p a t n -> p (a t) n")
                                      ).then_inc(history_in, 1)
                pool.wait_ge(z_ready, b * UNITS + i + 1)
                pool.wait_ge(history_in, b * UNITS + i + 1)
                settled()
                nc.gpsimd.tensor_copy(history[:, ds(i, 1), :, :].rearrange("p a t n -> p (a t) n"),
                                      z[:, :, COLS:COLS + 2]).then_inc(history_out, 1)

            nc.gpsimd.memset(ident[:, :], 0.0).then_inc(made, 1)
            pool.wait_ge(made, 3)
            nc.gpsimd.affine_select(out=ident[:, :], in_=ident[:, :], compare_op=ALU.not_equal, fill=1.0,
                                    base=0, pattern=[[-1, P]], channel_multiplier=1).then_inc(made, 1)
            pool.wait_ge(ws_loaded, 16)
            staged = staged_ws.rearrange("p (g s) -> p g s", g=GROUPS)
            nc.gpsimd.affine_select(out=staged, in_=staged, compare_op=ALU.is_ge, fill=0.0, base=0,
                                    pattern=[[0, GROUPS], [-1, P]], channel_multiplier=1).then_inc(made, 1)
            root(r_x, r_x_ready, everyone, 1)
            for dst, src in ((b_v, a_b_in[0, AW:2 * AW]), (b_s, a_b_s[0].rearrange("g t -> (g t)")),
                             (g_out, final_norm_g)):
                pool.dma_start(dst[:, :], src.partition_broadcast(P)).then_inc(consts, 16)
            load_rows(res, 0, res_loaded)
            pool.sem_inc(history_out, START)

            def block_norms(b, last):
                at = b * MEAN_BLOCK + 1
                root(r_v, r_v_ready, everyone, at + MEAN_V)
                for pair in range(2):
                    root(r_res, r_res_ready, slice(2 * pair, 2 * pair + 2), at + MEAN_RES + pair)
                pool.wait_ge(transposed, b * T_BLOCK + T_FIRST + KT)
                settled()
                load_rows(rows, b * COLS if last else (b + 1) * COLS, x_loaded)
                with pool.Fori(0, HALF_UNITS[0]) as i:
                    history_of(b, i)
                root(r_x, r_x_ready, everyone, at + MEAN_X)
                pool.wait_ge(r_x_ready, b + 2)
                settled()
                scale_x()
                with pool.Fori(HALF_UNITS[0], UNITS) as i:
                    history_of(b, i)
                for pair in range(2):
                    root(r_out, r_out_ready, slice(2 * pair, 2 * pair + 2), at + MEAN_OUT + pair)
                if last:
                    return
                pool.wait_ge(r_out_ready, b * 2 + START + 2)
                settled()
                for c in range(CH):
                    nc.gpsimd.tensor_scalar(res[:, c, :], res[:, c, :], r_out[:, c:c + 1], None,
                                            ALU.mult).then_inc(y_scaled, 1)
                    pool.wait_ge(y_scaled, b * CH + c + 1)
                    settled()
                    nc.gpsimd.tensor_tensor(res[:, c, :], res[:, c, :], g_out[:, :], ALU.mult).then_inc(y_done, 1)
                    pool.wait_ge(y_done, b * CH + c + 1)
                    settled()
                    pool.dma_start(out[0, ds(b * COLS + c * P, P), :], res[:, c, :]).then_inc(y_stored, 16)
                pool.wait_ge(y_stored, (b + 1) * (16 * CH))
                settled()
                load_rows(res, (b + 1) * COLS, res_loaded)

            with pool.Fori(0, BLOCKS - 1) as b:
                block_norms(b, False)
            block_norms(BLOCKS - 1, True)

        @block.tensor
        def _(pe):
            def part(pair, *at):
                return pair[0][at], pair[1][at]

            w, h, a = (w_hi, w_lo), (h_hi, h_lo), (a_hi, a_lo)
            everything = slice(None)

            def unit(b, mult, off, pairs, group, left, right, free, ready=None, after=None, beside=None,
                     by_bank=False):
                for q in range(pairs):
                    pe.wait_ge(w_ready, b * PAIRS + RAW + mult + off + q + 1)
                    if ready is not None:
                        ready(q)
                    slot = (off + q) % SPLIT
                    final = q == pairs - 1
                    order = [(t, n) for t in range(2) for n in range(4)]
                    if by_bank and final:
                        order = [(t, n) for n in range(4) for t in range(2)]
                    for i, (t, n) in enumerate(order):
                        k = 2 * q + t
                        if k == 0:
                            free(n)
                        last = product(ps[:, 4 * group + n, :], left(slot, t, k, n), right(slot, t, k, n),
                                       k == 0, k == 2 * pairs - 1,
                                       beside, q, 3 * i)
                        if by_bank and final and t == 1 and n < 3:
                            last.then_inc(bank_done, 1)
                    last.then_inc(w_used, 1)
                    if after is not None:
                        after(q)

            def rows_out(left_tiles):
                return (lambda slot, t, k, n: part(left_tiles, everything, k, slice(n * P, (n + 1) * P)),
                        lambda slot, t, k, n: part(w, everything, slot, t, everything))

            def features_out(right_tiles):
                return (lambda slot, t, k, n: part(w, everything, slot, t, slice(n * P, (n + 1) * P)),
                        lambda slot, t, k, n: part(right_tiles, everything, k, everything))

            def turn(k, bank):
                for c in range(CH):
                    last = nc.tensor.transpose(ps[:, bank, c * P:(c + 1) * P], rows[:, c, k * P:(k + 1) * P],
                                               ident[:, :])
                last.then_inc(transposed, 1)

            def turn_by_chunk(nth):
                for c in range(CH):
                    for k in range(KT):
                        if k == 0 or (c == 3 and k == 4):
                            if c % 2 == 0:
                                pe.wait_ge(rows_scaled_dve, nth * 5 + c + 2)
                            elif c == 1:
                                pe.wait_ge(rows_scaled_act, nth * 3 + 2)
                            elif k == 0:
                                pe.wait_ge(rows_scaled_dve, nth * 5 + 5)
                            else:
                                pe.wait_ge(rows_scaled_act, nth * 3 + 3)
                        last = nc.tensor.transpose(ps[:, k, c * P:(c + 1) * P], rows[:, c, k * P:(k + 1) * P],
                                                   ident[:, :])
                        if c == CH - 1:
                            last.then_inc(transposed, 1)

            def mix_pass(j, bank_free, chunk_ready=None):
                n, c, which = j // (2 * CH), j // 2 % CH, j % 2
                if n == 0 and which == 0:
                    chunk_ready(c)
                if c == 0 and which == 0:
                    bank_free(n)
                left = (a_hi, a_lo)[which][:, VS + c, n * P:(n + 1) * P]
                right = ws_split[:, c, :, :].rearrange("p h t -> p (h t)") if which == 0 else ws_split[:, c, 0, :]
                at = c % 2 * (2 * P)
                last = nc.tensor.matmul(ps[:, 4 + 2 * (n % 2) + c // 2, at:at + right.shape[-1]], left, right,
                                        start=which == 0, stop=which == 1)
                if j % (2 * CH) == 2 * CH - 1:
                    last.then_inc(mix_done, 1)

            def beside_pair(tiles, i, bank_free, chunk_ready=None):
                if i % 3 < 2:
                    mix_pass(tiles * (2 * CH) + i // 3 * 2 + i % 3, bank_free, chunk_ready)

            def product(out_ap, left, right, first, last, beside, q, i):
                for j, (l, r) in enumerate(((0, 0), (0, 1), (1, 0))):
                    if beside is not None:
                        beside(q, i + j)
                    mm = nc.tensor.matmul(out_ap, left[l], right[r], start=first and j == 0, stop=last and j == 2)
                return mm

            pe.sem_inc(w_used, SPLIT)
            pe.wait_ge(par_loaded, 16 * PARS)
            pe.wait_ge(made, 5)
            for i, n in enumerate((by_feature.shape[1], CONV_ROWS, CONV_ROWS)):
                last = nc.tensor.transpose(ps[:, 1, i * P:i * P + n], staged_par[0:n, i, :], ident[0:n, 0:n])
            last.then_inc(turned, 1)
            for g in range(GROUPS):
                last = nc.tensor.transpose(ps[:, 0, g * P:(g + 1) * P], staged_ws[:, g * P:(g + 1) * P], ident[:, :])
            last.then_inc(turned, 1)
            for _ in range(WARMING):
                nc.tensor.transpose(ps[:, 2, 0:P], ident[:, :], ident[:, :])
            pe.wait_ge(set_up, 4)
            turn_by_chunk(0)
            with pe.Fori(0, BLOCKS) as b:
                def drained(nth):
                    pe.wait_ge(dve_drained, b * DV_BLOCK + T_FIRST + nth)

                def act_has_drained(nth):
                    pe.wait_ge(act_drained, b * AC_BLOCK + nth)

                with pe.Fori(0, 2) as gg:
                    for par in range(2):
                        unit(b, gg * (2 * Q), V_PAIR + Q * par, Q, par, *rows_out(h),
                             free=lambda n: drained(gg * 8 + 4 * (par - 2) + n + 1),
                             ready=lambda q: drained(0) if q == 2 else None)
                with pe.Fori(0, 2) as half:
                    mult = half * HALF_PAIRS

                    def mix_free(g, n):
                        if n >= 2:
                            drained(half * 16 + DV[f"m{g}"] + n - 1)
                        elif g:
                            drained(half * 16 + DV["m0"] + n + 3)
                        else:
                            drained(half * 16 + DV["v3"] + 2 * n + 2)

                    def beside_u(g, q, i):
                        if q == Q - 1:
                            beside_pair(0, i, lambda n: mix_free(g, n), lambda c: mix_ready(g, c))
                        if g and q == 0:
                            beside_pair(2, i, lambda n: mix_free(0, n))

                    def mix_ready(g, c):
                        pe.wait_ge(vs_ready, b * (4 * GROUPS) + half * 8 + 4 * g + c + 1)
                        pe.wait_ge(ws_ready, b * (4 * GROUPS) + half * 8 + 4 * g + c + 1)

                    for g in range(2):
                        unit(b, mult, HALF_PAIR + Q * g, Q, 0, *features_out(h),
                             free=lambda n: act_has_drained(half * 8 + n + 1) if g else
                             drained(half * 16 + DV["v2"] + n + 1),
                             beside=lambda q, i: beside_u(g, q, i), by_bank=True)
                    for dh in range(2):
                        unit(b, mult, HALF_PAIR + Q * (2 + dh), Q, dh, *rows_out(a),
                             free=lambda n: drained(half * 16 + DV["m1"] + n // 2 + 3) if dh else
                             act_has_drained(half * 8 + 4 + n + 1),
                             ready=lambda q: pe.wait_ge(uv_ready, b * (4 * GROUPS) + half * 8 + UV_START + 2 * q + 2),
                             beside=None if dh else
                             lambda q, i: beside_pair(2, i, lambda n: mix_free(1, n)) if q == 0 else None,
                             by_bank=bool(dh))
                drained(DV["o11"] + 4)
                turn_by_chunk(b + 1)
                for half in range(2):
                    base = sum(HALF_UNITS[:half])

                    def up_free(i, par, n):
                        drained(DV["d01" if par else "d00"] + n + 1 if half else DV["T2"] + 4 * par + n + 1)
                        act_has_drained(i * 4 + (AC_UP + 4 * (base - 2)) + n + 1)

                    def up_unit(i, mult, par, off):
                        unit(b, mult, off, Q, par, *features_out(h),
                             free=lambda n: up_free(i, par, n),
                             ready=(lambda q: drained(DV["T2"] + 2 * q + 2) if q else None) if half == 0 else None)

                    with pe.Fori(0, HALF_UNITS[half] // 2) as i2:
                        for par in range(2):
                            up_unit(i2 * 2 + par, i2 * (2 * Q), par, UP_PAIR[half] + Q * par)
                    if HALF_UNITS[half] % 2:
                        i = HALF_UNITS[half] - 1
                        up_unit(i, 0, i % 2, UP_PAIR[half] + Q * i)

                    def first_turns(q):
                        if q == 2:
                            act_has_drained(AC_UP + 4 * UNITS)
                            pe.wait_ge(x_scaled, b * CH + CH)
                            for k in range(4):
                                turn(k, k)

                    for dh in range(2):
                        unit(b, 0, DOWN_PAIR[half] + dh * HALF_UNITS[half], HALF_UNITS[half], (half + dh) % 2,
                             *rows_out(a),
                             free=lambda n: drained(DV["T1a"] + n + 1) if half and dh else
                             act_has_drained(AC_UP + 4 * (UNITS - 2 if half else HALF_UNITS[0] - 2 + dh) + n + 1),
                             ready=lambda q: pe.wait_ge(gv_ready, b * UNITS + START + base + q + 1),
                             after=first_turns if half and dh == 0 else None, by_bank=bool(half and dh))
                drained(DV["d10"] + 4)
                for k in range(4, KT):
                    turn(k, k)


_INS = ['x', 'a_norm_g', 'a_w_in', 'a_b_in', 'a_v_norm_g', 'a_w_s', 'a_b_s', 'a_w_out',
        'ffn_norm_g', 'ffn_w_up', 'ffn_conv_w', 'ffn_conv_b', 'ffn_w_down', 'final_norm_g']


def kernel(**inputs):
    import numpy as _np
    import concourse.bacc as _bacc
    from concourse import mybir as _mybir
    from concourse.bass_utils import run_bass_kernel_spmd as _run

    nc = _bacc.Bacc("TRN2", target_bir_lowering=False, num_devices=1)
    arrays, args = {}, []
    for name in _INS:
        a = _np.ascontiguousarray(inputs[name])
        arrays[f"in_{name}_dram"] = a
        args.append(nc.dram_tensor(f"in_{name}_dram", a.shape, _mybir.dt.from_np(a.dtype), kind="ExternalInput").ap())
    out = nc.dram_tensor("out_0_dram", inputs['x'].shape, _mybir.dt.float32, kind="ExternalOutput").ap()
    gmlp_ffn_trunk(nc, *args, out)
    r = _run(nc, [arrays], core_ids=[0])
    return r.results[0]["out_0_dram"]
```
